# Optimizing a Trainium2 kernel written in Bass

```python
import jax, jax.numpy as jnp
from jax import lax
import numpy as np

D_MODEL = 1024
BATCH = 1
SEQ = 512
DEPTH = 1

CHUNK = 64
HEAD_DIM = 64
N_HEADS_A = 8
N_HEADS_B = 8
WIDTH_A = N_HEADS_A * HEAD_DIM
WIDTH_B = N_HEADS_B * HEAD_DIM
Q_BLOCK = 128
LEFT_CHUNKS = 8
BAND_CHUNKS = LEFT_CHUNKS + 1
BAND = BAND_CHUNKS * CHUNK
REL_CLIP = 128
N_REL = 2 * REL_CLIP + 1
D_FF = 2816
EPS = 1e-6
N_MOD = 9
FORGET_BIAS_CENTER = 3.0
NEG_INF = -1e30
IN_SIZES = (WIDTH_A, WIDTH_A, WIDTH_A, N_HEADS_A, WIDTH_B, WIDTH_B, WIDTH_B, D_MODEL, D_MODEL)
IN_COLS = sum(IN_SIZES)

kernel_name = "hybrid_fox_chunkrel_macaron_block"

def rms_norm(x, g):
    xf = x.astype(jnp.float32)
    y = xf * lax.rsqrt(jnp.mean(xf * xf, axis=-1, keepdims=True) + EPS)
    return (y * g.astype(jnp.float32)).astype(x.dtype)

def modulate(h, shift, scale):
    return h * (1.0 + scale[:, None, :]) + shift[:, None, :]

def swiglu(h, w_gate, w_up, w_down):
    return (jax.nn.silu(h @ w_gate) * (h @ w_up)) @ w_down

def forgetting_attention(q, k, v, log_f):
    B, S, H, dh = q.shape
    nb = S // Q_BLOCK
    F = jnp.cumsum(log_f, axis=1)
    F_k = F.transpose(0, 2, 1)
    q_blocks = q.reshape(B, nb, Q_BLOCK, H, dh).transpose(1, 0, 2, 3, 4)
    F_blocks = F.reshape(B, nb, Q_BLOCK, H).transpose(1, 0, 3, 2)
    starts = jnp.arange(nb, dtype=jnp.int32) * Q_BLOCK
    k_pos = jnp.arange(S, dtype=jnp.int32)
    scale = HEAD_DIM ** -0.5

    def one_block(args):
        qb, Fq, start = args
        s = jnp.einsum('bqhd,bkhd->bhqk', qb, k).astype(jnp.float32) * scale
        s = s + Fq[..., None] - F_k[:, :, None, :]
        q_pos = start + jnp.arange(Q_BLOCK, dtype=jnp.int32)
        mask = k_pos[None, :] <= q_pos[:, None]
        s = jnp.where(mask[None, None], s, NEG_INF)
        p = jax.nn.softmax(s, axis=-1).astype(v.dtype)
        return jnp.einsum('bhqk,bkhd->bqhd', p, v)

    out = lax.map(one_block, (q_blocks, F_blocks, starts))
    return out.transpose(1, 0, 2, 3, 4).reshape(B, S, H * dh)

def chunked_relpos_attention(q, k, v, rel_bias):
    B, S, H, dh = q.shape
    nc = S // CHUNK
    qc = q.reshape(B, nc, CHUNK, H, dh)
    pad = ((0, 0), (LEFT_CHUNKS, 0), (0, 0), (0, 0), (0, 0))
    kp = jnp.pad(k.reshape(B, nc, CHUNK, H, dh), pad)
    vp = jnp.pad(v.reshape(B, nc, CHUNK, H, dh), pad)
    k_band = jnp.concatenate([kp[:, j:j + nc] for j in range(BAND_CHUNKS)], axis=2)
    v_band = jnp.concatenate([vp[:, j:j + nc] for j in range(BAND_CHUNKS)], axis=2)
    s = jnp.einsum('bnqhd,bnkhd->bnhqk', qc, k_band).astype(jnp.float32) * (HEAD_DIM ** -0.5)
    qi = jnp.arange(CHUNK, dtype=jnp.int32)
    kj = jnp.arange(BAND, dtype=jnp.int32)
    dist = LEFT_CHUNKS * CHUNK + qi[:, None] - kj[None, :]
    idx = jnp.clip(dist, -REL_CLIP, REL_CLIP) + REL_CLIP
    bias = rel_bias.astype(jnp.float32)[:, idx]
    s = s + bias[None, None]
    chunk_ids = jnp.arange(nc, dtype=jnp.int32)[:, None] - LEFT_CHUNKS + jnp.arange(BAND_CHUNKS, dtype=jnp.int32)[None, :]
    key_valid = jnp.repeat(chunk_ids >= 0, CHUNK, axis=1)
    s = jnp.where(key_valid[None, :, None, None, :], s, NEG_INF)
    p = jax.nn.softmax(s, axis=-1).astype(v.dtype)
    out = jnp.einsum('bnhqk,bnkhd->bnqhd', p, v_band)
    return out.reshape(B, S, H * dh)

def token_mixing(h, w_in, forget_b, branch_gate_b, rel_bias, branch_w_a, branch_w_b, w_out):
    B, S, _ = h.shape
    proj = h @ w_in
    offs = np.cumsum((0,) + IN_SIZES)
    qa, ka, va, fa, qb, kb, vb, ga, gb = [proj[..., int(offs[i]):int(offs[i + 1])] for i in range(len(IN_SIZES))]
    heads = lambda t, n: t.reshape(B, S, n, HEAD_DIM)
    log_f = jax.nn.log_sigmoid(fa.astype(jnp.float32) + forget_b.astype(jnp.float32))
    y_a = forgetting_attention(heads(qa, N_HEADS_A), heads(ka, N_HEADS_A), heads(va, N_HEADS_A), log_f) @ branch_w_a
    y_b = chunked_relpos_attention(heads(qb, N_HEADS_B), heads(kb, N_HEADS_B), heads(vb, N_HEADS_B), rel_bias) @ branch_w_b
    g_a = jax.nn.sigmoid(ga + branch_gate_b[:D_MODEL])
    g_b = jax.nn.sigmoid(gb + branch_gate_b[D_MODEL:])
    return (g_a * y_a + g_b * y_b) @ w_out

def setup_inputs(seed: int = 0) -> dict:
    key = jax.random.key(seed)
    ks = jax.random.split(key, 24)
    nrm = lambda k, shape, s: jax.random.normal(k, shape, jnp.float32) * s
    L, D = DEPTH, D_MODEL
    return {
        "x": nrm(ks[0], (BATCH, SEQ, D), 1.0),
        "c": nrm(ks[1], (BATCH, D), 1.0),
        "ada_w": nrm(ks[2], (L, D, N_MOD * D), 0.5 * D ** -0.5),
        "ada_b": nrm(ks[3], (L, N_MOD * D), 0.02),
        "norm_ffn1": 1.0 + nrm(ks[4], (L, D), 0.05),
        "ffn1_w_gate": nrm(ks[5], (L, D, D_FF), D ** -0.5),
        "ffn1_w_up": nrm(ks[6], (L, D, D_FF), D ** -0.5),
        "ffn1_w_down": nrm(ks[7], (L, D_FF, D), D_FF ** -0.5),
        "norm_mix": 1.0 + nrm(ks[8], (L, D), 0.05),
        "mix_w_in": nrm(ks[9], (L, D, IN_COLS), D ** -0.5),
        "forget_b": FORGET_BIAS_CENTER + nrm(ks[10], (L, N_HEADS_A), 0.1),
        "branch_gate_b": nrm(ks[11], (L, 2 * D), 0.02),
        "rel_bias": nrm(ks[12], (L, N_HEADS_B, N_REL), 0.5),
        "branch_w_a": nrm(ks[13], (L, WIDTH_A, D), WIDTH_A ** -0.5),
        "branch_w_b": nrm(ks[14], (L, WIDTH_B, D), WIDTH_B ** -0.5),
        "mix_w_out": nrm(ks[15], (L, D, D), D ** -0.5),
        "norm_ffn2": 1.0 + nrm(ks[16], (L, D), 0.05),
        "ffn2_w_gate": nrm(ks[17], (L, D, D_FF), D ** -0.5),
        "ffn2_w_up": nrm(ks[18], (L, D, D_FF), D ** -0.5),
        "ffn2_w_down": nrm(ks[19], (L, D_FF, D), D_FF ** -0.5),
        "final_norm": 1.0 + nrm(ks[20], (D,), 0.05),
    }

def reference(x, c, ada_w, ada_b, norm_ffn1, ffn1_w_gate, ffn1_w_up, ffn1_w_down,
              norm_mix, mix_w_in, forget_b, branch_gate_b, rel_bias, branch_w_a, branch_w_b,
              mix_w_out, norm_ffn2, ffn2_w_gate, ffn2_w_up, ffn2_w_down, final_norm):
    c_act = jax.nn.silu(c)
    for l in range(DEPTH):
        mod = c_act @ ada_w[l] + ada_b[l]
        sh1, sc1, g1, sh2, sc2, g2, sh3, sc3, g3 = jnp.split(mod, N_MOD, axis=-1)
        h = modulate(rms_norm(x, norm_ffn1[l]), sh1, sc1)
        x = x + 0.5 * g1[:, None, :] * swiglu(h, ffn1_w_gate[l], ffn1_w_up[l], ffn1_w_down[l])
        h = modulate(rms_norm(x, norm_mix[l]), sh2, sc2)
        x = x + g2[:, None, :] * token_mixing(h, mix_w_in[l], forget_b[l], branch_gate_b[l], rel_bias[l],
                                              branch_w_a[l], branch_w_b[l], mix_w_out[l])
        h = modulate(rms_norm(x, norm_ffn2[l]), sh3, sc3)
        x = x + 0.5 * g3[:, None, :] * swiglu(h, ffn2_w_gate[l], ffn2_w_up[l], ffn2_w_down[l])
    return rms_norm(x, final_norm)


_drawn_inputs = setup_inputs


def setup_inputs(seed=0):
    import zlib

    import numpy as np

    out = dict(_drawn_inputs(seed))
    spreads = {}
    factors = {'ada_b': 4.029,
     'norm_ffn1': 7.643,
     'norm_mix': 8.0,
     'forget_b': 64.0,
     'branch_gate_b': 50.826,
     'rel_bias': 5.314,
     'norm_ffn2': 7.763}
    for name, (base, spread) in spreads.items():
        noise = np.random.default_rng([zlib.crc32(name.encode()), seed]).standard_normal(out[name].shape)
        drawn = base * np.exp(spread * noise) if base else spread * noise
        out[name] = __import__('jax').numpy.asarray(drawn.astype(out[name].dtype))
    for name, factor in factors.items():
        out[name] = (out[name] * factor).astype(out[name].dtype)
    return out
```

```python
from contextlib import ExitStack

import concourse.bass as bass
from concourse import mybir

ALU = mybir.AluOpType
ACT = mybir.ActivationFunctionType
F32 = mybir.dt.float32
F32R = mybir.dt.float32r
BF16 = mybir.dt.bfloat16
ds = bass.ds

P = 128
EPS = 1e-6
NEG_INF = -1e30
BIG = 3.0e38


def hybrid_block(nc, x, c, ada_w, ada_b, norm_ffn1, ffn1_w_gate, ffn1_w_up, ffn1_w_down,
                 norm_mix, mix_w_in, forget_b, branch_gate_b, rel_bias, branch_w_a, branch_w_b,
                 mix_w_out, norm_ffn2, ffn2_w_gate, ffn2_w_up, ffn2_w_down, final_norm, out):
    _, SEQ, D = x.shape
    DT = D // P
    TT = SEQ // P
    FF = ffn1_w_gate.shape[2]
    FT = FF // P
    HA = forget_b.shape[1]
    HB, N_REL = rel_bias.shape[1:]
    DH = 64
    WA, WB = HA * DH, HB * DH
    PAIRS = WA // P
    REL_CLIP = (N_REL - 1) // 2
    SCALE = DH ** -0.5
    N_MOD = ada_b.shape[1] // D
    UT = 8
    FREE = 2
    START = 1
    assert SEQ == 512 and DT == 8 and FT == 22 and WA == WB == 512 and REL_CLIP == 128

    PARTS = [(0, 8), (8, 8), (16, 6)]
    U_GU1 = 0
    U_DN1 = U_GU1 + 2 * FT
    U_FA = U_DN1 + 3 * DT
    U_MIX = [U_FA + 1, 0]
    U_BR = [U_MIX[0] + 5 * PAIRS, 0]
    U_MIX[1] = U_BR[0] + DT // 2
    U_BR[1] = U_MIX[1] + 5 * PAIRS
    U_OUT = U_BR[1] + DT // 2
    U_GU2 = U_OUT + DT
    U_DN2 = U_GU2 + 2 * FT
    U_END = U_DN2 + 3 * DT

    OFF_A = (0, WA, 2 * WA)
    OFF_F = 3 * WA
    OFF_B = (3 * WA + HA, 3 * WA + HA + WB, 3 * WA + HA + 2 * WB)
    OFF_G = 3 * WA + HA + 3 * WB
    QKV_OFF = (OFF_A, OFF_B)

    T_ORDER = (3, 2, 0, 1)
    T_OFF = {3: 0, 2: 512, 0: 896, 1: 1024}
    J_ORDER = (0, 1, 3, 2)
    J_OFF = {0: 0, 1: 512, 3: 896, 2: 1024}
    CW = 1280

    C_N1, C_NM, C_N2, C_AB, C_GB = 0, DT, 2 * DT, 3 * DT, 3 * DT + N_MOD * DT
    N_PRM = C_GB + 2 * DT
    M_SH = (0, 3 * DT, 6 * DT)
    M_SC = (DT, 4 * DT, 7 * DT)
    M_G = (2 * DT, 5 * DT, 8 * DT)

    ADA0, ADA1, ADA2 = 4, FT // 2, DT // 2
    AC, AC2 = 512, 384
    assert (ADA0 + ADA1) * AC + ADA2 * AC2 == N_MOD * D

    ctx = ExitStack()
    with ctx:
        def sb(name, shape, dt=F32, stack=ctx):
            return stack.enter_context(nc.sbuf_tensor(name, shape, dt))

        def sem(name):
            return ctx.enter_context(nc.semaphore(name))

        xT = sb("xT", [P, DT, SEQ])
        hH = sb("hH", [P, DT, SEQ], F32R)
        hL = sb("hL", [P, DT, SEQ], F32R)
        raw = [sb(f"raw{s}", [P, UT * P]) for s in range(2)]
        wH = [sb(f"wH{s}", [P, UT * P], F32R) for s in range(2)]
        wL = [sb(f"wL{s}", [P, UT * P], F32R) for s in range(2)]
        ident = sb("ident", [P, P])
        identb = sb("identb", [P, P], BF16)
        mask = [sb(f"mask{b}", [P, P], BF16) for b in range(2)]
        ones = sb("ones", [P, P])
        mhalf = sb("mhalf", [P, TT])
        prm_in = sb("prm_in", [P, P])
        prm = sb("prm", [P, P])
        mod = sb("mod", [P, N_MOD * DT])
        gs = sb("gs", [P, 3, DT])
        gres = sb("gres", [P, 3, DT])
        ccol = sb("ccol", [P, DT])
        csilu = sb("csilu", [P, DT])
        fb = sb("fb", [HA, 1])
        nfb = sb("nfb", [HA, 1])
        ssq0 = sb("ssq0", [P, TT])
        nrm = sb("nrm", [P, 5, TT])
        tmp = sb("tmp", [P, 2, SEQ])
        ssqa = sb("ssqa", [P, SEQ])
        diag = sb("diag", [P, TT, P])

        at_start = ExitStack()
        with at_start:
            xin = sb("xin", [P, TT, D], stack=at_start)
            sqx = sb("sqx", [P, D], stack=at_start)
        in_ffn = ExitStack()
        with in_ffn:
            actH = sb("actH", [P, FT, SEQ], F32R, stack=in_ffn)
            actL = sb("actL", [P, FT, SEQ], F32R, stack=in_ffn)
            sg = sb("sg", [P, 2, SEQ], stack=in_ffn)
            pr = sb("pr", [P, 2, SEQ], stack=in_ffn)
            adaw = sb("adaw", [P, 2, DT // 2, AC], stack=in_ffn)
            adac = sb("adac", [P, AC], stack=in_ffn)
        in_mix = ExitStack()
        with in_mix:
            gbuf = sb("gbuf", [P, DT, SEQ], stack=in_mix)
            oH = sb("oH", [P, PAIRS, SEQ], F32R, stack=in_mix)
            oL = sb("oL", [P, PAIRS, SEQ], F32R, stack=in_mix)
            ymix = sb("ymix", [P, DT, SEQ], stack=in_mix)
            prob = sb("prob", [P, 2, CW], stack=in_mix)
            ptH = sb("ptH", [P, CW], F32R, stack=in_mix)
            ptL = sb("ptL", [P, CW], F32R, stack=in_mix)
            qH = sb("qH", [P, SEQ], F32R, stack=in_mix)
            qL = sb("qL", [P, SEQ], F32R, stack=in_mix)
            kH = sb("kH", [P, SEQ], F32R, stack=in_mix)
            kL = sb("kL", [P, SEQ], F32R, stack=in_mix)
            vT = sb("vT", [P, SEQ], stack=in_mix)
            vH = sb("vH", [P, TT, P], F32R, stack=in_mix)
            vL = sb("vL", [P, TT, P], F32R, stack=in_mix)
            bias = sb("bias", [P, 2, SEQ], stack=in_mix)
            negmax = sb("negmax", [P, 2, TT], stack=in_mix)
            spare = sb("spare", [P, 2 * TT], stack=in_mix)
            rowsum = sb("rowsum", [P, 2, TT], stack=in_mix)
            rinv = sb("rinv", [P, 2, TT], stack=in_mix)
            fgate = sb("fgate", [HA, 6, SEQ], stack=in_mix)
            rel = sb("rel", [HB, N_REL], stack=in_mix)
            relx = sb("relx", [HB, SEQ + P], stack=in_mix)
        at_end = ExitStack()
        with at_end:
            gfin = sb("gfin", [P, D], stack=at_end)
            y = sb("y", [P, TT, D], stack=at_end)

        bank = ctx.enter_context(nc.psum_tensor("bank", [P, 8, SEQ], F32))
        B_ADA, B_BC, B_SSQ = 4, 4, 7
        S_BANK = (2, 5)

        negF_d = nc.dram_tensor("negF_d", [HA, SEQ], F32, kind="Internal").ap()
        relx_d = nc.dram_tensor("relx_d", [HB, SEQ + P], F32, kind="Internal").ap()
        relb_d = nc.dram_tensor("relb_d", [HB, P, SEQ], F32, kind="Internal").ap()

        raw_in = [sem(f"raw_in{s}") for s in range(2)]
        hi_done = sem("hi_done")
        lo_done = sem("lo_done")
        unit_done = sem("unit_done")
        c_in = sem("c_in")
        x_in = [sem(f"x_in{t}") for t in range(TT)]
        prm_loaded = sem("prm_loaded")
        fb_in = sem("fb_in")
        consts_v = sem("consts_v")
        ident_made = sem("ident_made")
        masks_made = sem("masks_made")
        identb_made = sem("identb_made")
        prm_T = sem("prm_T")
        prm_done = sem("prm_done")
        c_act = sem("c_act")
        xt_psum = sem("xt_psum")
        xt_done = sem("xt_done")
        ssq_x = sem("ssq_x")
        adaw_in = [sem(f"adaw_in{q}") for q in range(2)]
        adaw_used = [sem(f"adaw_used{q}") for q in range(2)]
        ada_step = sem("ada_step")
        ada_sum = sem("ada_sum")
        mod_done = sem("mod_done")
        gs_done = sem("gs_done")
        cols_done = sem("cols_done")
        ms_done = sem("ms_done")
        pow_done = sem("pow_done")
        newton = sem("newton")
        diag_done = sem("diag_done")
        bc_done = sem("bc_done")
        tmp_done = sem("tmp_done")
        hH_done = sem("hH_done")
        hL_done = sem("hL_done")
        ssq_ps = sem("ssq_ps")
        silu_done = [[sem(f"silu{n}_{j}") for j in range(2)] for n in range(2)]
        prod_done = [[sem(f"prod{n}_{j}") for j in range(2)] for n in range(2)]
        actH_done = [sem(f"actH_done{n}") for n in range(2)]
        actL_done = [sem(f"actL_done{n}") for n in range(2)]
        x_done = [[sem(f"x_done{n}_{j}") for j in range(2)] for n in range(3)]
        sq_done = [sem(f"sq_done{n}") for n in range(3)]
        ssqa_done = [sem(f"ssqa_done{n}") for n in range(3)]
        d_free = [sem(f"d_free{b}") for b in range(2)]
        fa_sem = sem("fa_sem")
        fa_act = sem("fa_act")
        negF_done = sem("negF_done")
        negF_out = sem("negF_out")
        rel_in = sem("rel_in")
        relx_done = sem("relx_done")
        relx_out = sem("relx_out")
        relb_out = sem("relb_out")
        bias_in = sem("bias_in")
        qhi = sem("qhi")
        v_copied = sem("v_copied")
        v_turned = sem("v_turned")
        vhi = sem("vhi")
        s_done = sem("s_done")
        biased = sem("biased")
        exp_done = sem("exp_done")
        rinv_done = sem("rinv_done")
        p_ready = sem("p_ready")
        p_turned = sem("p_turned")
        pthi = sem("pthi")
        pt_ready = sem("pt_ready")
        pv_done = sem("pv_done")
        ohi = [sem(f"ohi{h}") for h in range(2)]
        o_ready = [sem(f"o_ready{h}") for h in range(2)]
        gates_done = sem("gates_done")
        y_done = sem("y_done")
        yadd_done = sem("yadd_done")
        yhi = sem("yhi")
        yH_ready = sem("yH_ready")
        gfin_in = sem("gfin_in")
        yt_done = sem("yt_done")
        y_ready = sem("y_ready")
        out_sent = sem("out_sent")

        def f32(ap):
            return ap.bitcast(F32)

        def landed(base, stride, i, k):
            return 16 * ((base + k) // 2 + 1) + i * (8 * stride)

        def tiles_of(w, cols, n=UT, k0=0):
            return w.rearrange("a (k p) n -> p (a k) n", p=P)[:, k0:k0 + n, cols]

        def sp_load(sp, base, stride, i, k, src):
            s = (base + k) % 2
            n, w = src.shape[1], src.shape[2]
            sp.wait_ge(lo_done, base + k - 1 + FREE + i * stride)
            sp.dma_start(raw[s][:, :n * w].rearrange("p (k n) -> p k n", k=n), src).then_inc(raw_in[s], 16)

        def sp_ada(sp, done, i, q, col, width):
            sp.wait_ge(adaw_used[q], done + i + START)
            src = ada_w.rearrange("a (p k) n -> p (a k) n", k=DT)[:, 4 * q:4 * q + 4, ds(col, width)]
            sp.dma_start(adaw[:, q, :, :width], src).then_inc(adaw_in[q], 16)

        def sp_ffn(sp, w_gate, w_up, w_down, u_gu, u_dn, ada):
            with sp.Fori(0, FT // 2) as i:
                for k in range(4):
                    w = (w_gate, w_up)[k % 2]
                    sp_load(sp, u_gu, 4, i, k, tiles_of(w, ds(i * 2 * P + (k // 2) * P, P)))
                    if ada and k < 2:
                        sp_ada(sp, ADA0, i, k, i * AC + ADA0 * AC, AC)
            with sp.Fori(0, DT // 2) as i:
                for k in range(6):
                    k0, n = PARTS[k % 3]
                    sp_load(sp, u_dn, 6, i, k, tiles_of(w_down, ds(i * 2 * P + (k // 3) * P, P), n, k0))
                    if ada and k < 2:
                        sp_ada(sp, ADA0 + ADA1, i, k, i * AC2 + (ADA0 + ADA1) * AC, AC2)

        def sp_pairs(sp, br):
            offs = QKV_OFF[br]
            src_bias = (negF_d, relb_d)[br]
            with sp.Fori(0, PAIRS // 2) as i:
                for pp in range(2):
                    for k in range(5):
                        if k < 3:
                            cols = ds(i * 2 * P + offs[k] + pp * P, P)
                        else:
                            cols = ds(i * 4 * P + OFF_G + br * D + (2 * pp + k - 3) * P, P)
                        sp_load(sp, U_MIX[br], 10, i, 5 * pp + k, tiles_of(mix_w_in, cols))
                        if k == 2:
                            sp.wait_ge((negF_out, relb_out)[br], 16)
                            sp.wait_ge(biased, i * 16 + 8 * (4 * br + pp) + START)
                            if br == 0:
                                src = src_bias[ds(i * 4 + 2 * pp, 2), :].partition_broadcast(P)
                            else:
                                src = src_bias.rearrange("h p s -> p h s")[:, ds(i * 4 + 2 * pp, 2), :]
                            sp.dma_start(bias[:, :, :], src).then_inc(bias_in, 16)

        def sp_branch(sp, br):
            w = (branch_w_a, branch_w_b)[br]
            with sp.Fori(0, DT // 4) as i:
                for k in range(2):
                    sp_load(sp, U_BR[br], 2, i, k, tiles_of(w, ds(i * 4 * P + k * 2 * P, 2 * P), 4))

        block = ctx.enter_context(nc.Block())

        @block.sync
        def _(sp):
            sp.dma_start(ccol[:, :], c.rearrange("a (p k) -> p (a k)", k=DT)).then_inc(c_in, 16)
            row = 0
            for src in (norm_ffn1, norm_mix, norm_ffn2, ada_b, branch_gate_b):
                n = src.shape[1] // P
                sp.dma_start(prm_in[row:row + n, :], src.rearrange("a (r n) -> (a r) n", n=P)).then_inc(prm_loaded, 16)
                row += n
            sp.dma_start(fb[:, :], forget_b.rearrange("a h -> h a")).then_inc(fb_in, 16)
            for t in range(TT):
                sp.dma_start(xin[:, t, :], x[0, t * P:(t + 1) * P, :]).then_inc(x_in[t], 16)
            with sp.Fori(0, ADA0) as i:
                for q in range(2):
                    sp_ada(sp, 0, i, q, i * AC, AC)
            sp_ffn(sp, ffn1_w_gate, ffn1_w_up, ffn1_w_down, U_GU1, U_DN1, True)
            sp_load(sp, U_FA, 0, 0, 0, tiles_of(mix_w_in, slice(OFF_F, OFF_F + P)))
            sp_pairs(sp, 0)
            sp_branch(sp, 0)
            sp_pairs(sp, 1)
            sp_branch(sp, 1)
            with sp.Fori(0, DT // 2) as i:
                for k in range(2):
                    sp_load(sp, U_OUT, 2, i, k, tiles_of(mix_w_out, ds(i * 2 * P + k * P, P)))
            sp_ffn(sp, ffn2_w_gate, ffn2_w_up, ffn2_w_down, U_GU2, U_DN2, False)
            sp.wait_ge(unit_done, U_END)
            sp.dma_start(gfin[:, :], final_norm.rearrange("(a n) -> a n", a=1).partition_broadcast(P)).then_inc(gfin_in, 16)
            for t in range(TT):
                sp.wait_ge(y_ready, 2 * (t + 1))
                sp.dma_start(out[0, t * P:(t + 1) * P, :], y[:, t, :]).then_inc(out_sent, 16)
            sp.wait_ge(out_sent, 16 * TT)

        @block.gpsimd
        def _(pool):
            pool.wait_ge(consts_v, 5)
            nc.gpsimd.affine_select(out=ident[:, :], in_=ident[:, :], compare_op=ALU.not_equal, fill=1.0, base=0,
                                    pattern=[[-1, P]], channel_multiplier=1).then_inc(ident_made, 1)
            nc.gpsimd.affine_select(out=mask[0][:, :], in_=mask[0][:, :], compare_op=ALU.is_ge, fill=NEG_INF, base=0,
                                    pattern=[[-1, P]], channel_multiplier=1).then_inc(masks_made, 1)
            for n in range(4):
                pool.wait_ge(ms_done, n + 1)
                nc.gpsimd.tensor_tensor(nrm[:, 1, :], nrm[:, 0, :], mhalf[:, :], ALU.pow).then_inc(pow_done, 1)
                if n == 1:
                    pool.wait_ge(unit_done, U_FA)
                    pool.dma_start(rel[:, :], rel_bias[0, :, :]).then_inc(rel_in, 16)
                    pool.wait_ge(relx_done, 2)
                    pool.dma_start(relx_d, relx[:, :]).then_inc(relx_out, 16)
                    pool.wait_ge(relx_out, 16)
                    pool.dma_start(relb_d, bass.AP(relx_d.tensor, P, [[SEQ + P, HB], [-1, P], [1, SEQ]])).then_inc(relb_out, 16)
                    pool.wait_ge(negF_done, 1)
                    pool.dma_start(negF_d, fgate[:, 5, :]).then_inc(negF_out, 16)

        @block.scalar
        def _(act):
            def wait_apart(s, v):
                act.wait_ge(s, v)

            def prep(base, stride, i, k, n=UT):
                u = base + k
                if u >= U_END:
                    return
                s = u % 2
                act.wait_ge(raw_in[s], landed(base, stride, i, k))
                if u >= 2:
                    act.wait_ge(unit_done, u - 1 + i * stride)
                nc.scalar.activation(wH[s][:, :n * P], raw[s][:, :n * P], ACT.Copy).then_inc(hi_done, 1)

            def normed(n):
                for d in range(DT):
                    act.wait_ge(tmp_done, n * DT + d + 1)
                    nc.scalar.activation(hH[:, d, :], tmp[:, d % 2, :], ACT.Identity,
                                         bias=mod[:, M_SH[n] + d:M_SH[n] + d + 1]).then_inc(hH_done, 1)

            def gate_up(n, u0):
                with act.Fori(0, FT // 2) as i:
                    for k in range(4):
                        prep(u0, 4, i, k + 2)
                        j = k // 2
                        if k % 2 == 0:
                            act.wait_ge(prod_done[n][j], i + START)
                            act.wait_ge(unit_done, i * 4 + u0 + k + 1)
                            nc.scalar.activation(sg[:, j, :], bank[:, k, :], ACT.Silu).then_inc(silu_done[n][j], 1)
                        else:
                            wait_apart(prod_done[n][j], i + 1 + START)
                            nc.scalar.activation(actH[:, ds(i * 2 + j, 1), :], pr[:, j:j + 1, :], ACT.Copy).then_inc(actH_done[n], 1)

            def squares(m, j, i):
                act.wait_ge(ssqa_done[m], i * 2 + j + START)
                wait_apart(x_done[m][j], i + 1 + START)
                nc.scalar.activation(tmp[:, j:j + 1, :], xT[:, ds(i * 2 + j, 1), :], ACT.Square).then_inc(sq_done[m], 1)

            def down(n, m, u0):
                def body(i):
                    for k in range(6):
                        if not (isinstance(i, int) and n == 1 and k >= 4):
                            prep(u0, 6, i, k + 2, PARTS[(k + 2) % 3][1])
                        if k % 3 == 2:
                            squares(m, k // 3, i)
                with act.Fori(0, DT // 2 - n) as i:
                    body(i)
                if n == 1:
                    body(DT // 2 - 1)

            def pairs(br):
                u0 = U_MIX[br]
                if br == 1:
                    act.wait_ge(y_done, DT + START)
                with act.Fori(0, PAIRS // 2) as i:
                    for pp in range(2):
                        g = i * 2 + (4 * br + pp)
                        k0 = 5 * pp
                        for k, dst, sc in ((0, qH, SCALE), (1, kH, 1.0)):
                            prep(u0, 10, i, k0 + k + 2)
                            act.wait_ge(s_done, g * 8 + START)
                            act.wait_ge(unit_done, i * 10 + u0 + k0 + k + 1)
                            nc.scalar.activation(dst[:, :], bank[:, k, :], ACT.Copy, scale=sc).then_inc(qhi, 1)
                        prep(u0, 10, i, k0 + 4)
                        act.wait_ge(unit_done, i * 10 + u0 + k0 + 3)
                        nc.scalar.activation(vT[:, :], bank[:, 0, :], ACT.Copy).then_inc(v_copied, 1)
                        for h in range(2):
                            for n, t in enumerate(T_ORDER):
                                w = P * (t + 1)
                                act.wait_ge(biased, g * 8 + (4 * h + n + 1) + START)
                                nc.scalar.activation(prob[:, h, T_OFF[t]:T_OFF[t] + w], prob[:, h, T_OFF[t]:T_OFF[t] + w],
                                                     ACT.Exp, scale=-1.0, bias=negmax[:, h, t:t + 1],
                                                     accum_out=rowsum[:, h, t:t + 1]).then_inc(exp_done, 1)
                            if h == 0:
                                act.wait_ge(v_turned, g + 1)
                                nc.scalar.activation(vH[:, :, :], bank[:, 1, :].rearrange("p (a b) -> p a b", a=TT),
                                                     ACT.Copy).then_inc(vhi, 1)

                        def gate(n):
                            wait_apart(unit_done, i * 10 + u0 + k0 + 4 + n)
                            col = i * 4 + C_GB + br * DT + 2 * pp + n
                            nc.scalar.activation(gbuf[:, ds(i * 4 + 2 * pp + n, 1), :], bank[:, n:n + 1, :], ACT.Identity,
                                                 bias=prm[:, ds(col, 1)]).then_inc(d_free[n], 1)

                        def turned_hi(h):
                            act.wait_ge(pv_done, g * 2 + h + START)
                            act.wait_ge(p_turned, g * 2 + h + 1)
                            sbk = S_BANK[h]
                            nc.scalar.activation(ptH[:, :], bank[:, sbk:sbk + 3, :].rearrange("p a b -> p (a b)")[:, :CW],
                                                 ACT.Copy).then_inc(pthi, 1)

                        def out_hi(h):
                            wait_apart(pv_done, g * 2 + h + 1 + START)
                            rows = slice(DH * h, DH * h + DH)
                            nc.scalar.activation(oH[rows, ds(i * 2 + pp, 1), :], bank[rows, S_BANK[h]:S_BANK[h] + 1, :],
                                                 ACT.Copy).then_inc(ohi[h], 1)

                        prep(u0, 10, i, k0 + 5)
                        gate(0)
                        turned_hi(0)
                        out_hi(0)
                        turned_hi(1)
                        prep(u0, 10, i, k0 + 6)
                        gate(1)
                        out_hi(1)

            def branch(br):
                act.wait_ge(d_free[0], 1 + 2 * PAIRS * (br + 1))
                act.wait_ge(d_free[1], 3 * PAIRS * (br + 1) + START)
                for d in range(DT):
                    nc.scalar.activation(gbuf[:, d, :], gbuf[:, d, :], ACT.Sigmoid).then_inc(gates_done, 1)
                with act.Fori(0, DT // 4) as i:
                    for k in range(2):
                        prep(U_BR[br], 2, i, k + 2)

            for first in silu_done[0] + silu_done[1]:
                act.sem_inc(first, START)
            act.wait_ge(c_in, 16)
            nc.scalar.activation(csilu[:, :], ccol[:, :], ACT.Silu).then_inc(c_act, 1)
            act.wait_ge(prm_T, 1)
            nc.scalar.activation(prm[:, :N_PRM], bank[:, 0, :N_PRM], ACT.Copy).then_inc(prm_done, 1)
            for d in range(DT):
                act.wait_ge(xt_psum, d + 1)
                nc.scalar.activation(xT[:, d, :], bank[:, 1 + d % 2, :], ACT.Copy).then_inc(xt_done, 1)
            for t in range(TT):
                if t >= 1:
                    act.wait_ge(ssq_x, t)
                nc.scalar.activation(sqx[:, :], xin[:, t, :], ACT.Square, accum_out=ssq0[:, t:t + 1]).then_inc(ssq_x, 1)
            for k in range(2):
                prep(0, 0, 0, k)
            normed(0)
            gate_up(0, U_GU1)
            down(0, 0, U_DN1)
            normed(1)
            prep(U_FA, 0, 0, 2)
            act.wait_ge(unit_done, U_FA + 1)
            nc.scalar.activation(fgate[:, 0, :], bank[0:HA, 0, :], ACT.Abs, bias=fb[:, :]).then_inc(fa_act, 1)
            nc.scalar.activation(fgate[:, 3, :], bank[0:HA, 0, :], ACT.Relu, bias=nfb[:, :], scale=-1.0).then_inc(d_free[0], 1)
            act.wait_ge(fa_act, 1)
            nc.scalar.activation(fgate[:, 1, :], fgate[:, 0, :], ACT.Exp, scale=-1.0).then_inc(fa_act, 1)
            act.wait_ge(fa_act, 2)
            nc.scalar.activation(fgate[:, 2, :], fgate[:, 1, :], ACT.Ln, bias=1.0).then_inc(fa_act, 1)
            pairs(0)
            branch(0)
            pairs(1)
            branch(1)
            for d in range(DT):
                act.wait_ge(yadd_done, d + 1)
                nc.scalar.activation(hH[:, d, :], ymix[:, d, :], ACT.Copy).then_inc(yhi, 1)
            with act.Fori(0, DT // 2) as i:
                for k in range(2):
                    prep(U_OUT, 2, i, k + 2)
                    squares(1, k, i)
            normed(2)
            gate_up(1, U_GU2)
            down(1, 2, U_DN2)

        @block.vector
        def _(dve):
            V = nc.vector

            def wait_apart(s, v, at):
                dve.wait_ge(s, v)
                V.memset(at, 0.0)

            def prep(base, stride, i, k, n=UT):
                u = base + k
                if u >= U_END:
                    return
                s = u % 2
                dve.wait_ge(hi_done, u + 1 + i * stride)
                V.tensor_tensor(wL[s][:, :n * P], raw[s][:, :n * P], f32(wH[s][:, :n * P]), ALU.subtract).then_inc(lo_done, 1)

            def ada_half(done, i, q, width):
                dve.wait_ge(adaw_in[q], i * 16 + 16 * (done + 1))
                for r in range(4):
                    k = 4 * q + r
                    if k == 0:
                        ins = V.tensor_scalar(adac[:, :width], adaw[:, q, r, :width], csilu[:, 0:1], None, ALU.mult)
                    else:
                        dve.wait_ge(ada_step, i * 8 + (8 * done + k))
                        ins = V.scalar_tensor_tensor(out=adac[:, :width], in0=adaw[:, q, r, :width], scalar=csilu[:, k:k + 1],
                                                     in1=adac[:, :width], op0=ALU.mult, op1=ALU.add)
                    ins.then_inc(ada_step, 1)
                dve.wait_ge(ada_step, i * 8 + (8 * done + 4 * q + 4))
                dve.sem_inc(adaw_used[q], 1)

            def ada_mod(done, i, col, nt):
                dve.wait_ge(ada_sum, i + (done + 1))
                V.tensor_tensor(mod[:, ds(col, nt)], bank[:, B_ADA, 0:nt], prm[:, ds(col + C_AB, nt)], ALU.add).then_inc(mod_done, 1)

            def rstd(n):
                if n == 0:
                    dve.wait_ge(ssq_x, TT)
                    src = ssq0[:, :]
                else:
                    dve.wait_ge(ssq_ps, n)
                    src = bank[:, B_SSQ, 0:TT]
                V.tensor_scalar(nrm[:, 0, :], src, 1.0 / D, EPS, ALU.mult, ALU.add).then_inc(ms_done, 1)
                dve.wait_ge(pow_done, n + 1)
                V.scalar_tensor_tensor(out=nrm[:, 2, :], in0=nrm[:, 1, :], scalar=-0.5, in1=nrm[:, 1, :],
                                       op0=ALU.mult, op1=ALU.mult).then_inc(newton, 1)
                dve.wait_ge(newton, 3 * n + 1)
                V.tensor_tensor(nrm[:, 3, :], nrm[:, 2, :], nrm[:, 0, :], ALU.mult).then_inc(newton, 1)
                dve.wait_ge(newton, 3 * n + 2)
                V.scalar_tensor_tensor(out=nrm[:, 4, :], in0=nrm[:, 3, :], scalar=1.5, in1=nrm[:, 1, :],
                                       op0=ALU.add, op1=ALU.mult).then_inc(newton, 1)
                dve.wait_ge(newton, 3 * n + 3)

            def normed(n):
                rstd(n)
                V.tensor_tensor(diag[:, :, :], ident[:, :].rearrange("p (a b) -> p a b", a=1).to_broadcast([P, TT, P]),
                                nrm[:, 4, :].rearrange("p (a b) -> p a b", b=1).to_broadcast([P, TT, P]),
                                ALU.mult).then_inc(diag_done, 1)
                dve.wait_ge(bc_done, n + 1)
                dve.wait_ge(gs_done, n + 1)
                if n == 0:
                    dve.wait_ge(xt_done, DT)

                def scaled(d):
                    V.scalar_tensor_tensor(out=tmp[:, d % 2, :], in0=xT[:, d, :], scalar=gs[:, n, d:d + 1],
                                           in1=bank[:, B_BC, :], op0=ALU.mult, op1=ALU.mult).then_inc(tmp_done, 1)

                scaled(0)
                for d in range(DT):
                    if d + 1 < DT:
                        if d >= 1:
                            dve.wait_ge(hL_done, n * DT + d)
                        scaled(d + 1)
                    dve.wait_ge(hH_done, n * DT + d + 1)
                    V.scalar_tensor_tensor(out=hL[:, d, :], in0=tmp[:, d % 2, :], scalar=mod[:, M_SH[n] + d:M_SH[n] + d + 1],
                                           in1=f32(hH[:, d, :]), op0=ALU.add, op1=ALU.subtract).then_inc(hL_done, 1)

            def scale_columns(n, g_col):
                V.scalar_tensor_tensor(out=gs[:, n, :], in0=mod[:, M_SC[n]:M_SC[n] + DT], scalar=1.0,
                                       in1=prm[:, g_col:g_col + DT], op0=ALU.add, op1=ALU.mult).then_inc(gs_done, 1)

            def gate_up(n, u0, ada):
                with dve.Fori(0, FT // 2) as i:
                    for k in range(4):
                        j = k // 2
                        if k % 2:
                            dve.wait_ge(silu_done[n][j], i + 1 + START)
                            dve.wait_ge(unit_done, i * 4 + u0 + k + 1)
                            dve.wait_ge(actL_done[n], i * 2 + START)
                            V.tensor_tensor(pr[:, j, :], sg[:, j, :], bank[:, k, :], ALU.mult).then_inc(prod_done[n][j], 1)
                        prep(u0, 4, i, k + 2)
                        if k % 2:
                            dve.wait_ge(actH_done[n], i * 2 + j + 1)
                            V.tensor_tensor(actL[:, ds(i * 2 + j, 1), :], pr[:, j:j + 1, :], f32(actH[:, ds(i * 2 + j, 1), :]),
                                            ALU.subtract).then_inc(actL_done[n], 1)
                        if ada and k in (1, 2):
                            ada_half(ADA0, i, k - 1, AC)
                        if ada and k == 3:
                            ada_mod(ADA0, i, i * (AC // P) + ADA0 * (AC // P), AC // P)

            def residual(m, j, i, b, u):
                dve.wait_ge(unit_done, u)
                V.scalar_tensor_tensor(out=xT[:, ds(i * 2 + j, 1), :], in0=bank[:, b:b + 1, :],
                                       scalar=gres[:, m, ds(i * 2 + j, 1)], in1=xT[:, ds(i * 2 + j, 1), :],
                                       op0=ALU.mult, op1=ALU.add).then_inc(x_done[m][j], 1)

            def add_squares(m, j, i):
                dve.wait_ge(sq_done[m], i * 2 + j + 1)
                dve.wait_ge(ssqa_done[m], i * 2 + j + START)
                V.tensor_tensor(ssqa[:, :], ssqa[:, :], tmp[:, j, :], ALU.add).then_inc(ssqa_done[m], 1)

            def down(n, m, u0, ada):
                def body(i):
                    for k in range(6):
                        if k % 3 == 2:
                            residual(m, k // 3, i, 5 + k // 3, i * 6 + u0 + k + 1)
                        if not (isinstance(i, int) and n == 1 and k >= 4):
                            prep(u0, 6, i, k + 2, PARTS[(k + 2) % 3][1])
                        if k % 3 == 2:
                            add_squares(m, k // 3, i)
                        if ada and k in (1, 3):
                            ada_half(ADA0 + ADA1, i, k // 2, AC2)
                        if ada and k == 5:
                            ada_mod(ADA0 + ADA1, i, i * (AC2 // P) + (ADA0 + ADA1) * (AC // P), AC2 // P)
                with dve.Fori(0, DT // 2 - n) as i:
                    body(i)
                if n == 1:
                    body(DT // 2 - 1)

            def pairs(br):
                u0 = U_MIX[br]
                with dve.Fori(0, PAIRS // 2) as i:
                    for pp in range(2):
                        g = i * 2 + (4 * br + pp)
                        k0 = 5 * pp
                        dve.wait_ge(qhi, g * 2 + 1)
                        V.scalar_tensor_tensor(out=qL[:, :], in0=bank[:, 0, :], scalar=SCALE, in1=f32(qH[:, :]),
                                               op0=ALU.mult, op1=ALU.subtract).then_inc(d_free[0], 1)
                        prep(u0, 10, i, k0 + 2)
                        dve.wait_ge(qhi, g * 2 + 2)
                        V.tensor_tensor(kL[:, :], bank[:, 1, :], f32(kH[:, :]), ALU.subtract).then_inc(d_free[1], 1)
                        prep(u0, 10, i, k0 + 3)
                        prep(u0, 10, i, k0 + 4)

                        def biased_scores(h):
                            for n, t in enumerate(T_ORDER):
                                w = P * (t + 1)
                                b0 = (0, SEQ - w)[br]
                                if n == 0:
                                    dve.wait_ge(bias_in, g * 16 + 16)
                                wait_apart(s_done, g * 8 + (4 * h + (1, 3, 3, 4)[n]) + START, spare[:, 4 * h + n:4 * h + n + 1])
                                V.tensor_tensor_reduce(
                                    out=prob[:, h, T_OFF[t]:T_OFF[t] + w],
                                    in0=bank[:, S_BANK[h]:S_BANK[h] + 3, :].rearrange("p a b -> p (a b)")[:, T_OFF[t]:T_OFF[t] + w],
                                    in1=bias[:, h, b0:b0 + w], scale=-1.0, scalar=BIG, op0=ALU.add, op1=ALU.min,
                                    accum_out=negmax[:, h, t:t + 1]).then_inc(biased, 1)

                        def normalised(h):
                            dve.wait_ge(exp_done, g * 8 + (4 * h + 4))
                            V.reciprocal(rinv[:, h, :], rowsum[:, h, :]).then_inc(rinv_done, 1)
                            dve.wait_ge(rinv_done, g * 2 + h + 1)
                            for n, t in enumerate(T_ORDER):
                                a = prob[:, h, T_OFF[t]:T_OFF[t] + P * (t + 1)]
                                V.tensor_scalar(a, a, rinv[:, h, t:t + 1], None, ALU.mult).then_inc(p_ready, 1)

                        def turned_lo(h):
                            dve.wait_ge(pthi, g * 2 + h + 1)
                            V.tensor_tensor(ptL[:, :], bank[:, S_BANK[h]:S_BANK[h] + 3, :].rearrange("p a b -> p (a b)")[:, :CW],
                                            f32(ptH[:, :]), ALU.subtract).then_inc(pt_ready, 1)

                        def out_lo(h):
                            rows = slice(DH * h, DH * h + DH)
                            dve.wait_ge(ohi[h], g + 1)
                            V.tensor_tensor(oL[rows, ds(i * 2 + pp, 1), :], bank[rows, S_BANK[h]:S_BANK[h] + 1, :],
                                            f32(oH[rows, ds(i * 2 + pp, 1), :]), ALU.subtract).then_inc(o_ready[h], 1)

                        biased_scores(0)
                        biased_scores(1)
                        normalised(0)
                        dve.wait_ge(vhi, g + 1)
                        V.tensor_tensor(vL[:, :, :], bank[:, 1, :].rearrange("p (a b) -> p a b", a=TT), f32(vH[:, :, :]),
                                        ALU.subtract).then_inc(d_free[1], 1)
                        normalised(1)
                        prep(u0, 10, i, k0 + 5)
                        turned_lo(0)
                        out_lo(0)
                        turned_lo(1)
                        prep(u0, 10, i, k0 + 6)
                        out_lo(1)

            def branch(br):
                u0 = U_BR[br]
                dve.wait_ge(gates_done, DT * (br + 1))
                with dve.Fori(0, DT // 4) as i:
                    for k in range(2):
                        dve.wait_ge(unit_done, i * 2 + u0 + k + 1)
                        for e in range(2):
                            t = ds(i * 4 + 2 * k + e, 1)
                            if br == 0:
                                V.tensor_tensor(ymix[:, t, :], bank[:, 2 + 2 * k + e:3 + 2 * k + e, :], gbuf[:, t, :],
                                                ALU.mult).then_inc(y_done, 1)
                            else:
                                V.tensor_tensor(gbuf[:, t, :], bank[:, 2 + 2 * k + e:3 + 2 * k + e, :], gbuf[:, t, :],
                                                ALU.mult).then_inc(y_done, 1)
                        if br == 1:
                            for e in range(2):
                                t = ds(i * 4 + 2 * k + e, 1)
                                dve.wait_ge(y_done, i * 4 + DT + 2 * k + e + 1 + START)
                                V.tensor_tensor(ymix[:, t, :], ymix[:, t, :], gbuf[:, t, :], ALU.add).then_inc(yadd_done, 1)
                        prep(u0, 2, i, k + 2)

            dve.sem_inc(lo_done, FREE)
            for first in (prod_done[0] + prod_done[1] + adaw_used + [mod_done] + x_done[0] + x_done[1] + x_done[2]
                          + actL_done + ssqa_done + [biased, d_free[1], y_done] + o_ready):
                dve.sem_inc(first, START)
            V.memset(ident[:, :], 0.0).then_inc(consts_v, 1)
            V.memset(mask[0][:, :], 0.0).then_inc(consts_v, 1)
            V.memset(mask[1][:, :], 0.0).then_inc(consts_v, 1)
            V.memset(ones[:, :], 1.0).then_inc(consts_v, 1)
            V.memset(mhalf[:, :], -0.5).then_inc(consts_v, 1)
            dve.wait_ge(consts_v, 3)
            V.memset(mask[1][0:64, 64:P], NEG_INF).then_inc(masks_made, 1)
            dve.wait_ge(ident_made, 1)
            V.tensor_copy(identb[:, :], ident[:, :]).then_inc(identb_made, 1)
            dve.wait_ge(fb_in, 16)
            V.tensor_scalar(nfb[:, :], fb[:, :], -1.0, None, ALU.mult).then_inc(fa_sem, 1)
            dve.wait_ge(c_act, 1)
            dve.wait_ge(prm_done, 1)
            with dve.Fori(0, ADA0) as i:
                ada_half(0, i, 0, AC)
                ada_half(0, i, 1, AC)
                ada_mod(0, i, i * (AC // P), AC // P)
            dve.wait_ge(mod_done, ADA0 + START)
            scale_columns(0, C_N1)
            for k in range(2):
                prep(0, 0, 0, k)
            normed(0)
            gate_up(0, U_GU1, True)
            dve.wait_ge(mod_done, ADA0 + ADA1 + START)
            V.tensor_scalar(gres[:, 0, :], mod[:, M_G[0]:M_G[0] + DT], 0.5, None, ALU.mult).then_inc(cols_done, 1)
            scale_columns(1, C_NM)
            V.tensor_copy(gres[:, 1, :], mod[:, M_G[1]:M_G[1] + DT]).then_inc(cols_done, 1)
            V.memset(ssqa[:, :], 0.0).then_inc(cols_done, 1)
            dve.wait_ge(cols_done, 3)
            down(0, 0, U_DN1, True)
            dve.wait_ge(mod_done, ADA0 + ADA1 + ADA2 + START)
            scale_columns(2, C_N2)
            V.tensor_scalar(gres[:, 2, :], mod[:, M_G[2]:M_G[2] + DT], 0.5, None, ALU.mult).then_inc(cols_done, 1)
            normed(1)
            prep(U_FA, 0, 0, 2)
            dve.wait_ge(fa_act, 3)
            dve.wait_ge(d_free[0], 1)
            z = fgate
            V.tensor_scalar(z[:, 0, :], z[:, 1, :], 1.0, -1.0, ALU.add, ALU.add).then_inc(fa_sem, 1)
            dve.wait_ge(fa_sem, 2)
            V.tensor_scalar(z[:, 4, :], z[:, 0, :], 1e-30, None, ALU.max).then_inc(fa_sem, 1)
            dve.wait_ge(fa_sem, 3)
            V.reciprocal(z[:, 5, :], z[:, 4, :]).then_inc(fa_sem, 1)
            dve.wait_ge(fa_sem, 4)
            V.tensor_tensor(z[:, 4, :], z[:, 5, :], z[:, 2, :], ALU.mult).then_inc(fa_sem, 1)
            dve.wait_ge(fa_sem, 5)
            V.scalar_tensor_tensor(out=z[:, 5, :], in0=z[:, 0, :], scalar=0.0, in1=z[:, 4, :],
                                   op0=ALU.is_equal, op1=ALU.add).then_inc(fa_sem, 1)
            dve.wait_ge(fa_sem, 6)
            V.tensor_tensor(z[:, 4, :], z[:, 5, :], z[:, 1, :], ALU.mult).then_inc(fa_sem, 1)
            dve.wait_ge(fa_sem, 7)
            V.tensor_tensor(z[:, 0, :], z[:, 4, :], z[:, 3, :], ALU.add).then_inc(fa_sem, 1)
            dve.wait_ge(fa_sem, 8)
            V.tensor_tensor_scan(z[:, 5, :], ones[0:HA, 0:1].to_broadcast([HA, SEQ]), z[:, 0, :], 0.0,
                                 ALU.mult, ALU.add).then_inc(negF_done, 1)
            dve.wait_ge(rel_in, 16)
            half = SEQ + P - (N_REL - 1)
            V.tensor_copy(relx[:, :half], rel[:, N_REL - 1:N_REL].to_broadcast([HB, half])).then_inc(relx_done, 1)
            V.tensor_copy(relx[:, half:], rel[:, N_REL - 1:0:-1]).then_inc(relx_done, 1)
            V.memset(ssqa[:, :], 0.0).then_inc(cols_done, 1)
            pairs(0)
            branch(0)
            pairs(1)
            branch(1)
            for d in range(DT):
                dve.wait_ge(yhi, d + 1)
                V.tensor_tensor(hL[:, d, :], ymix[:, d, :], f32(hH[:, d, :]), ALU.subtract).then_inc(yH_ready, 1)
            with dve.Fori(0, DT // 2) as i:
                for k in range(2):
                    residual(1, k, i, 2 + k, i * 2 + U_OUT + k + 1)
                    prep(U_OUT, 2, i, k + 2)
                    add_squares(1, k, i)
            normed(2)
            gate_up(1, U_GU2, False)
            V.memset(ssqa[:, :], 0.0).then_inc(cols_done, 1)
            dve.wait_ge(cols_done, 6)
            down(1, 2, U_DN2, False)
            rstd(3)
            dve.wait_ge(gfin_in, 16)
            for t in range(TT):
                for e in range(2):
                    dve.wait_ge(yt_done, 2 * t + e + 1)
                    cols = slice(e * SEQ, (e + 1) * SEQ)
                    V.scalar_tensor_tensor(out=y[:, t, cols], in0=bank[:, (2 * t + e) % 4, :], scalar=nrm[:, 4, t:t + 1],
                                           in1=gfin[:, cols], op0=ALU.mult, op1=ALU.mult).then_inc(y_ready, 1)

        @block.tensor
        def _(pe):
            T = nc.tensor

            def three(o, a, b, start, stop):
                T.matmul(o, a[0], b[0], start=start, stop=False)
                T.matmul(o, a[0], b[1], start=False, stop=False)
                return T.matmul(o, a[1], b[0], start=False, stop=stop)

            def tile(s, k):
                return wH[s][:, k * P:(k + 1) * P], wL[s][:, k * P:(k + 1) * P]

            def dense(u, s, o, rhs, ks, first, last, at=0):
                if at == 0:
                    pe.wait_ge(lo_done, u + 1 + FREE)
                for n, k in enumerate(ks):
                    ins = three(o, tile(s, at + n), (rhs[0][:, k, :], rhs[1][:, k, :]), first and n == 0,
                                last and n == len(ks) - 1)
                return ins

            h = (hH, hL)
            a = (actH, actL)
            o_ = (oH, oL)

            def h_unit(u, s, o, ks=range(DT), ready=None):
                if ready is None:
                    return dense(u, s, o, h, ks, ks[0] == 0, ks[-1] == DT - 1, ks[0])
                pe.wait_ge(lo_done, u + 1 + FREE)
                for k in ks:
                    pe.wait_ge(hL_done, ready + k + 1)
                    ins = three(o, tile(s, k), (hH[:, k, :], hL[:, k, :]), k == 0, k == DT - 1)
                return ins

            def ada_sums(done, i, nt):
                pe.wait_ge(ada_step, i * 8 + 8 * (done + 1))
                pe.wait_ge(mod_done, i + done + START)
                for n in range(nt):
                    ins = T.matmul(bank[:, B_ADA, n:n + 1], adac[:, n * P:(n + 1) * P], ones[:, 0:1], start=True, stop=True)
                ins.then_inc(ada_sum, 1)

            def token_squares(m):
                pe.wait_ge(ssqa_done[m], DT + START)
                for t in range(TT):
                    ins = T.matmul(bank[:, B_SSQ, t:t + 1], ssqa[:, t * P:(t + 1) * P], ones[:, 0:1], start=True, stop=True)
                ins.then_inc(ssq_ps, 1)

            def spread(n):
                pe.wait_ge(diag_done, n + 1)
                for t in range(TT):
                    ins = T.matmul(bank[:, B_BC, t * P:(t + 1) * P], ones[:, :], diag[:, t, :], start=True, stop=True)
                ins.then_inc(bc_done, 1)

            def gate_up(n, u0, ready, ada):
                with pe.Fori(0, FT // 2) as i:
                    for k in range(4):
                        pe.wait_ge((silu_done, prod_done)[k % 2][n][k // 2], i + START)
                        h_unit(i * 4 + u0 + k, (u0 + k) % 2, bank[:, k, :], ready=ready if k == 0 else None).then_inc(unit_done, 1)
                    if ada:
                        ada_sums(ADA0, i, AC // P)

            def down(n, m, u0, ada):
                with pe.Fori(0, DT // 2) as i:
                    for k in range(6):
                        k0, cnt = PARTS[k % 3]
                        j = k // 3
                        if k % 3 == 0:
                            pe.wait_ge(x_done[m][j], i + START)
                        pe.wait_ge(actL_done[n], k0 + cnt + START)
                        u = i * 6 + u0 + k
                        pe.wait_ge(lo_done, u + 1 + FREE)
                        for q in range(cnt):
                            f = k0 + q
                            ins = three(bank[:, 5 + j, :], tile((u0 + k) % 2, q), (actH[:, f, :], actL[:, f, :]),
                                        f == 0, f == FT - 1)
                        ins.then_inc(unit_done, 1)
                    if ada:
                        ada_sums(ADA0 + ADA1, i, AC2 // P)

            def pairs(br):
                u0 = U_MIX[br]
                if br == 1:
                    pe.wait_ge(y_done, DT + START)
                with pe.Fori(0, PAIRS // 2) as i:
                    for pp in range(2):
                        g = i * 2 + (4 * br + pp)
                        k0 = 5 * pp

                        def unit(k, b, ks=range(DT)):
                            return h_unit(i * 10 + u0 + k0 + k, (u0 + k0 + k) % 2, bank[:, b, :], ks)

                        def flat(hh):
                            return bank[:, S_BANK[hh]:S_BANK[hh] + 3, :].rearrange("p a b -> p (a b)")

                        def scores(hh):
                            rows = slice(DH * hh, DH * hh + DH)
                            pe.wait_ge(o_ready[hh], g + START)
                            for t in T_ORDER:
                                w = P * (t + 1)
                                o = flat(hh)[:, T_OFF[t]:T_OFF[t] + w]
                                three(o, (qH[rows, t * P:(t + 1) * P], qL[rows, t * P:(t + 1) * P]),
                                      (kH[rows, :w], kL[rows, :w]), True, False)
                                T.matmul(o[:, w - P:w], identb[:, :], mask[br][:, :], start=False, stop=True).then_inc(s_done, 1)

                        def turn(hh):
                            pe.wait_ge(p_ready, g * 8 + (4 * hh + 4))
                            for j in J_ORDER:
                                for t in range(j, TT):
                                    ins = T.transpose(flat(hh)[:, J_OFF[j] + (t - j) * P:J_OFF[j] + (t - j + 1) * P],
                                                      prob[:, hh, T_OFF[t] + j * P:T_OFF[t] + (j + 1) * P], ident[:, :])
                            ins.then_inc(p_turned, 1)

                        def values(hh):
                            pe.wait_ge(d_free[1], g * 3 + 2 + START)
                            pe.wait_ge(pt_ready, g * 2 + hh + 1)
                            for j in range(TT):
                                w = SEQ - j * P
                                o = bank[:, S_BANK[hh], j * P:SEQ]
                                ins = three(o, (vH[:, j, :], vL[:, j, :]),
                                            (ptH[:, J_OFF[j]:J_OFF[j] + w], ptL[:, J_OFF[j]:J_OFF[j] + w]), j == 0, j == TT - 1)
                            ins.then_inc(pv_done, 1)

                        pe.wait_ge(d_free[0], g * 2 + 1)
                        unit(0, 0).then_inc(unit_done, 1)
                        pe.wait_ge(d_free[1], g * 3 + START)
                        unit(1, 1).then_inc(unit_done, 1)
                        pe.wait_ge(d_free[0], g * 2 + 2)
                        unit(2, 0).then_inc(unit_done, 1)
                        pe.wait_ge(d_free[1], g * 3 + 1 + START)
                        scores(0)
                        scores(1)
                        pe.wait_ge(v_copied, g + 1)
                        for t in range(TT):
                            ins = T.transpose(bank[:, 1, t * P:(t + 1) * P], vT[:, t * P:(t + 1) * P], ident[:, :])
                        ins.then_inc(v_turned, 1)
                        unit(3, 0).then_inc(unit_done, 1)
                        turn(0)
                        pe.wait_ge(d_free[1], g * 3 + 2 + START)
                        unit(4, 1, range(0, DT // 2))
                        values(0)
                        turn(1)
                        unit(4, 1, range(DT // 2, DT)).then_inc(unit_done, 1)
                        values(1)

            def branch(br):
                u0 = U_BR[br]
                for hh in range(2):
                    pe.wait_ge(o_ready[hh], PAIRS * (br + 1) + START)
                with pe.Fori(0, DT // 4) as i:
                    for k in range(2):
                        s = (u0 + k) % 2
                        pe.wait_ge(y_done, i * 4 + br * DT + START)
                        pe.wait_ge(lo_done, i * 2 + u0 + k + 1 + FREE)
                        for e in range(2):
                            for q in range(PAIRS):
                                cols = slice((q * 2 + e) * P, (q * 2 + e + 1) * P)
                                ins = three(bank[:, 2 + 2 * k + e, :], (wH[s][:, cols], wL[s][:, cols]),
                                            (oH[:, q, :], oL[:, q, :]), q == 0, q == PAIRS - 1)
                        ins.then_inc(unit_done, 1)

            for first in (s_done, pv_done):
                pe.sem_inc(first, START)
            pe.wait_ge(ident_made, 1)
            pe.wait_ge(prm_loaded, 16 * 5)
            T.transpose(bank[:, 0, :N_PRM], prm_in[:N_PRM, :], ident[:N_PRM, :N_PRM]).then_inc(prm_T, 1)
            for t in range(TT):
                pe.wait_ge(x_in[t], 16)
            for d in range(DT):
                if d >= 2:
                    pe.wait_ge(xt_done, d - 1)
                for t in range(TT):
                    ins = T.transpose(bank[:, 1 + d % 2, t * P:(t + 1) * P], xin[:, t, d * P:(d + 1) * P], ident[:, :])
                ins.then_inc(xt_psum, 1)
            with pe.Fori(0, ADA0) as i:
                ada_sums(0, i, AC // P)
            spread(0)
            gate_up(0, U_GU1, 0, True)
            down(0, 0, U_DN1, True)
            token_squares(0)
            spread(1)
            h_unit(U_FA, U_FA % 2, bank[:, 0, :], ready=DT).then_inc(unit_done, 1)
            pe.wait_ge(identb_made, 1)
            pe.wait_ge(masks_made, 2)
            pairs(0)
            branch(0)
            pairs(1)
            branch(1)
            with pe.Fori(0, DT // 2) as i:
                for k in range(2):
                    pe.wait_ge(x_done[1][k], i + START)
                    if k == 0:
                        pe.wait_ge(y_done, 2 * DT + START)
                        pe.wait_ge(lo_done, i * 2 + U_OUT + k + 1 + FREE)
                        for q in range(DT):
                            pe.wait_ge(yH_ready, q + 1)
                            ins = three(bank[:, 2 + k, :], tile((U_OUT + k) % 2, q), (hH[:, q, :], hL[:, q, :]),
                                        q == 0, q == DT - 1)
                    else:
                        ins = h_unit(i * 2 + U_OUT + k, (U_OUT + k) % 2, bank[:, 2 + k, :])
                    ins.then_inc(unit_done, 1)
            token_squares(1)
            spread(2)
            gate_up(1, U_GU2, 2 * DT, False)
            down(1, 2, U_DN2, False)
            token_squares(2)
            for t in range(TT):
                for e in range(2):
                    n = 2 * t + e
                    if n >= 4:
                        pe.wait_ge(y_ready, n - 3)
                    for q in range(4):
                        ins = T.transpose(bank[:, n % 4, q * P:(q + 1) * P], xT[:, 4 * e + q, t * P:(t + 1) * P], ident[:, :])
                    ins.then_inc(yt_done, 1)


_INS = ['x', 'c', 'ada_w', 'ada_b', 'norm_ffn1', 'ffn1_w_gate', 'ffn1_w_up', 'ffn1_w_down', 'norm_mix', 'mix_w_in',
        'forget_b', 'branch_gate_b', 'rel_bias', 'branch_w_a', 'branch_w_b', 'mix_w_out', 'norm_ffn2', 'ffn2_w_gate',
        'ffn2_w_up', 'ffn2_w_down', 'final_norm']
_OUTS = [((1, 512, 1024), 'float32')]


def kernel(**inputs):
    import numpy as _np
    import concourse.bacc as _bacc
    from concourse import mybir as _mybir
    from concourse.bass_utils import run_bass_kernel_spmd as _run

    nc = _bacc.Bacc("TRN2", target_bir_lowering=False, num_devices=1)
    arrays, args = {}, []
    for name in _INS:
        a = _np.ascontiguousarray(inputs[name])
        arrays[f"in_{name}_dram"] = a
        args.append(nc.dram_tensor(f"in_{name}_dram", a.shape, _mybir.dt.from_np(a.dtype), kind="ExternalInput").ap())
    for i, (shape, dtype) in enumerate(_OUTS):
        dt = _mybir.dt.from_np(_np.dtype(dtype))
        args.append(nc.dram_tensor(f"out_{i}_dram", shape, dt, kind="ExternalOutput").ap())
    hybrid_block(nc, *args)
    r = _run(nc, [arrays], core_ids=[0])
    return r.results[0]["out_0_dram"]
```

```python
from contextlib import ExitStack

import concourse.bass as bass
from concourse import mybir

ALU = mybir.AluOpType
ACT = mybir.ActivationFunctionType
F32 = mybir.dt.float32
F32R = mybir.dt.float32r
BF16 = mybir.dt.bfloat16
ds = bass.ds

P = 128
EPS = 1e-6
NEG_INF = -1e30
BIG = 3.0e38


def hybrid_block(nc, x, c, ada_w, ada_b, norm_ffn1, ffn1_w_gate, ffn1_w_up, ffn1_w_down,
                 norm_mix, mix_w_in, forget_b, branch_gate_b, rel_bias, branch_w_a, branch_w_b,
                 mix_w_out, norm_ffn2, ffn2_w_gate, ffn2_w_up, ffn2_w_down, final_norm, out):
    _, SEQ, D = x.shape
    DT = D // P
    TT = SEQ // P
    FF = ffn1_w_gate.shape[2]
    FT = FF // P
    HA = forget_b.shape[1]
    HB, N_REL = rel_bias.shape[1:]
    DH = 64
    WA, WB = HA * DH, HB * DH
    PAIRS = WA // P
    REL_CLIP = (N_REL - 1) // 2
    SCALE = DH ** -0.5
    N_MOD = ada_b.shape[1] // D
    UT = 8
    FREE = 2
    START = 1
    Y_START = START + 2
    assert SEQ == 512 and DT == 8 and FT == 22 and WA == WB == 512 and REL_CLIP == 128

    PARTS = [(0, 8), (8, 8), (16, 6)]
    U_GU1 = 0
    U_DN1 = U_GU1 + 2 * FT
    U_FA = U_DN1 + 3 * DT
    U_MIX = [U_FA + 1, 0]
    U_BR = [U_MIX[0] + 5 * PAIRS, 0]
    U_MIX[1] = U_BR[0] + DT // 2
    U_BR[1] = U_MIX[1] + 5 * PAIRS
    U_OUT = U_BR[1] + DT // 2
    U_GU2 = U_OUT + DT
    U_DN2 = U_GU2 + 2 * FT
    U_END = U_DN2 + 3 * DT

    OFF_A = (0, WA, 2 * WA)
    OFF_F = 3 * WA
    OFF_B = (3 * WA + HA, 3 * WA + HA + WB, 3 * WA + HA + 2 * WB)
    OFF_G = 3 * WA + HA + 3 * WB
    QKV_OFF = (OFF_A, OFF_B)

    T_ORDER = (3, 2, 0, 1)
    T_OFF = {3: 0, 2: 512, 0: 896, 1: 1024}
    J_PIECES = ((0,), (1, 3, 2))
    PIECE_COLS = (slice(0, 512), slice(512, 1280))
    J_OFF = {0: 0, 1: 512, 3: 896, 2: 1024}
    CW = 1280

    C_N1, C_NM, C_N2, C_AB, C_GB = 0, DT, 2 * DT, 3 * DT, 3 * DT + N_MOD * DT
    C_NF = C_GB + 2 * DT
    N_PRM = C_NF + DT
    M_SH = (0, 3 * DT, 6 * DT)
    M_SC = (DT, 4 * DT, 7 * DT)
    M_G = (2 * DT, 5 * DT, 8 * DT)

    ADA0, ADA1, ADA2 = 4, FT // 2, DT // 2
    AC, AC2 = 512, 384
    assert (ADA0 + ADA1) * AC + ADA2 * AC2 == N_MOD * D

    ctx = ExitStack()
    with ctx:
        def sb(name, shape, dt=F32, stack=ctx):
            return stack.enter_context(nc.sbuf_tensor(name, shape, dt))

        def sem(name):
            return ctx.enter_context(nc.semaphore(name))

        xT = sb("xT", [P, DT, SEQ])
        hH = sb("hH", [P, DT, SEQ], F32R)
        hL = sb("hL", [P, DT, SEQ], F32R)
        raw = [sb(f"raw{s}", [P, UT * P]) for s in range(2)]
        wH = [sb(f"wH{s}", [P, UT * P], F32R) for s in range(2)]
        wL = [sb(f"wL{s}", [P, UT * P], F32R) for s in range(2)]
        ident = sb("ident", [P, P])
        identb = sb("identb", [P, P], BF16)
        mask = [sb(f"mask{b}", [P, P], BF16) for b in range(2)]
        ones = sb("ones", [P, P])
        mhalf = sb("mhalf", [P, TT])
        prm_in = sb("prm_in", [P, P])
        prm = sb("prm", [P, P])
        mod = sb("mod", [P, N_MOD * DT])
        gs = sb("gs", [P, 3, DT])
        gres = sb("gres", [P, 3, DT])
        ccol = sb("ccol", [P, DT])
        csilu = sb("csilu", [P, DT])
        fb = sb("fb", [HA, 1])
        nfb = sb("nfb", [HA, 1])
        ssq0 = sb("ssq0", [P, TT])
        nrm = sb("nrm", [P, 5, TT])
        tmp = sb("tmp", [P, 2, SEQ])
        ssqa = sb("ssqa", [P, SEQ])
        diag = sb("diag", [P, TT, P])

        at_start = ExitStack()
        with at_start:
            xin = sb("xin", [P, TT, D], stack=at_start)
            sqx = sb("sqx", [P, D], stack=at_start)
            adas = sb("adas", [P, ADA0, DT, AC], stack=at_start)
            adasc = sb("adasc", [P, ADA0, AC], stack=at_start)
        in_ffn = ExitStack()
        with in_ffn:
            actH = sb("actH", [P, FT, SEQ], F32R, stack=in_ffn)
            actL = sb("actL", [P, FT, SEQ], F32R, stack=in_ffn)
            sg = sb("sg", [P, 2, SEQ], stack=in_ffn)
            pr = sb("pr", [P, 2, SEQ], stack=in_ffn)
            adaw = sb("adaw", [P, 2, DT // 2, AC], stack=in_ffn)
            adac = sb("adac", [P, AC], stack=in_ffn)
        in_mix = ExitStack()
        with in_mix:
            gbuf = sb("gbuf", [P, DT, SEQ], stack=in_mix)
            oH = sb("oH", [P, PAIRS, SEQ], F32R, stack=in_mix)
            oL = sb("oL", [P, PAIRS, SEQ], F32R, stack=in_mix)
            ymix = sb("ymix", [P, DT, SEQ], stack=in_mix)
            prob = sb("prob", [P, 2, CW], stack=in_mix)
            ptH = sb("ptH", [P, CW], F32R, stack=in_mix)
            ptL = sb("ptL", [P, CW], F32R, stack=in_mix)
            qH = sb("qH", [P, SEQ], F32R, stack=in_mix)
            qL = sb("qL", [P, SEQ], F32R, stack=in_mix)
            kH = sb("kH", [P, SEQ], F32R, stack=in_mix)
            kL = sb("kL", [P, SEQ], F32R, stack=in_mix)
            vT = sb("vT", [P, SEQ], stack=in_mix)
            vH = sb("vH", [P, TT, P], F32R, stack=in_mix)
            vL = sb("vL", [P, TT, P], F32R, stack=in_mix)
            bias = sb("bias", [P, 2, SEQ], stack=in_mix)
            negmax = sb("negmax", [P, 2, TT], stack=in_mix)
            spare = sb("spare", [P, 2 * TT], stack=in_mix)
            rowsum = sb("rowsum", [P, 2, TT], stack=in_mix)
            rinv = sb("rinv", [P, 2, TT], stack=in_mix)
            fgate = sb("fgate", [HA, 6, SEQ], stack=in_mix)
            rel = sb("rel", [HB, N_REL], stack=in_mix)
            relx = sb("relx", [HB, SEQ + P], stack=in_mix)
        xg = adaw[:, :, :, :].rearrange("p a b n -> p (a b) n")
        at_end = ExitStack()
        with at_end:
            y = sb("y", [P, TT, D], stack=at_end)

        bank = ctx.enter_context(nc.psum_tensor("bank", [P, 8, SEQ], F32))
        B_ADA, B_BC, B_SSQ, B_FA = 4, 4, 7, 7
        B_ADA_START = (3, 5, 6, 7)
        Y_BANK = (0, 1, 2, 3, 4, 5, 0, 1)
        S_BANK = (2, 5)

        negF_d = nc.dram_tensor("negF_d", [HA, SEQ], F32, kind="Internal").ap()
        relx_d = nc.dram_tensor("relx_d", [HB, SEQ + P], F32, kind="Internal").ap()
        relb_d = nc.dram_tensor("relb_d", [HB, P, SEQ], F32, kind="Internal").ap()

        raw_in = [sem(f"raw_in{s}") for s in range(2)]
        hi_done = sem("hi_done")
        lo_done = sem("lo_done")
        unit_done = sem("unit_done")
        c_in = sem("c_in")
        x_in = [sem(f"x_in{t}") for t in range(TT)]
        prm_loaded = sem("prm_loaded")
        fb_in = sem("fb_in")
        consts_v = sem("consts_v")
        ident_made = sem("ident_made")
        masks_made = sem("masks_made")
        identb_made = sem("identb_made")
        prm_T = sem("prm_T")
        prm_done = sem("prm_done")
        c_act = sem("c_act")
        xt_psum = sem("xt_psum")
        xt_done = sem("xt_done")
        ssq_x = sem("ssq_x")
        adas_in = [[sem(f"adas_in{b}_{q}") for q in range(2)] for b in range(ADA0)]
        adas_step = sem("adas_step")
        adas_sum = sem("adas_sum")
        mod_first = sem("mod_first")
        adaw_in = [sem(f"adaw_in{q}") for q in range(2)]
        adaw_used = [sem(f"adaw_used{q}") for q in range(2)]
        ada_step = sem("ada_step")
        ada_sum = sem("ada_sum")
        mod_done = sem("mod_done")
        gs_done = sem("gs_done")
        cols_done = sem("cols_done")
        ms_done = sem("ms_done")
        pow_done = sem("pow_done")
        newton = sem("newton")
        diag_done = sem("diag_done")
        bc_done = sem("bc_done")
        tmp_done = sem("tmp_done")
        hH_done = sem("hH_done")
        hL_done = sem("hL_done")
        ssq_ps = sem("ssq_ps")
        silu_done = [[sem(f"silu{n}_{j}") for j in range(2)] for n in range(2)]
        prod_done = [[sem(f"prod{n}_{j}") for j in range(2)] for n in range(2)]
        actH_done = [sem(f"actH_done{n}") for n in range(2)]
        actL_done = [sem(f"actL_done{n}") for n in range(2)]
        x_done = [[sem(f"x_done{n}_{j}") for j in range(2)] for n in range(3)]
        sq_done = [sem(f"sq_done{n}") for n in range(3)]
        ssqa_done = [sem(f"ssqa_done{n}") for n in range(3)]
        d_free = [sem(f"d_free{b}") for b in range(2)]
        fa_sem = sem("fa_sem")
        fa_act = sem("fa_act")
        negF_done = sem("negF_done")
        negF_out = sem("negF_out")
        rel_in = sem("rel_in")
        relx_done = sem("relx_done")
        relx_out = sem("relx_out")
        relb_out = sem("relb_out")
        bias_in = sem("bias_in")
        qhi = sem("qhi")
        v_copied = sem("v_copied")
        v_turned = sem("v_turned")
        vhi = sem("vhi")
        s_done = sem("s_done")
        biased = sem("biased")
        exp_done = sem("exp_done")
        rinv_done = sem("rinv_done")
        p_ready = sem("p_ready")
        p_turned = sem("p_turned")
        pthi = sem("pthi")
        pt_ready = sem("pt_ready")
        pv_done = sem("pv_done")
        ohi = [sem(f"ohi{h}") for h in range(2)]
        o_ready = [sem(f"o_ready{h}") for h in range(2)]
        gates_done = sem("gates_done")
        y_done = sem("y_done")
        yadd_done = sem("yadd_done")
        yhi = sem("yhi")
        yH_ready = sem("yH_ready")
        xg_done = sem("xg_done")
        yt_done = sem("yt_done")
        y_ready = [sem(f"y_ready{e}") for e in range(2)]
        out_sent = sem("out_sent")

        def f32(ap):
            return ap.bitcast(F32)

        def landed(base, stride, i, k):
            return 16 * ((base + k) // 2 + 1) + i * (8 * stride)

        def tiles_of(w, cols, n=UT, k0=0):
            return w.rearrange("a (k p) n -> p (a k) n", p=P)[:, k0:k0 + n, cols]

        def sp_load(sp, base, stride, i, k, src):
            s = (base + k) % 2
            n, w = src.shape[1], src.shape[2]
            sp.wait_ge(lo_done, base + k - 1 + FREE + i * stride)
            sp.dma_start(raw[s][:, :n * w].rearrange("p (k n) -> p k n", k=n), src).then_inc(raw_in[s], 16)

        def sp_ada(sp, done, i, q, col, width):
            sp.wait_ge(adaw_used[q], done + i + START)
            src = ada_w.rearrange("a (p k) n -> p (a k) n", k=DT)[:, 4 * q:4 * q + 4, ds(col, width)]
            sp.dma_start(adaw[:, q, :, :width], src).then_inc(adaw_in[q], 16)

        def sp_ffn(sp, w_gate, w_up, w_down, u_gu, u_dn, ada):
            def gate_up(i, k0):
                for k in range(k0, 4):
                    w = (w_gate, w_up)[k % 2]
                    sp_load(sp, u_gu, 4, i, k, tiles_of(w, ds(i * 2 * P + (k // 2) * P, P)))
                    if ada and k >= 2:
                        sp_ada(sp, 0, i, k - 2, i * AC + ADA0 * AC, AC)

            if ada:
                gate_up(0, 2)
            with sp.Fori(int(ada), FT // 2) as i:
                gate_up(i, 0)
            with sp.Fori(0, DT // 2) as i:
                for k in range(6):
                    k0, n = PARTS[k % 3]
                    sp_load(sp, u_dn, 6, i, k, tiles_of(w_down, ds(i * 2 * P + (k // 3) * P, P), n, k0))
                    if ada and k < 2:
                        sp_ada(sp, ADA1, i, k, i * AC2 + (ADA0 + ADA1) * AC, AC2)

        def sp_pairs(sp, br):
            offs = QKV_OFF[br]
            src_bias = (negF_d, relb_d)[br]
            with sp.Fori(0, PAIRS // 2) as i:
                for pp in range(2):
                    for k in range(5):
                        if k < 3:
                            cols = ds(i * 2 * P + offs[k] + pp * P, P)
                        else:
                            cols = ds(i * 4 * P + OFF_G + br * D + (2 * pp + k - 3) * P, P)
                        sp_load(sp, U_MIX[br], 10, i, 5 * pp + k, tiles_of(mix_w_in, cols))
                        if k == 2:
                            sp.wait_ge((negF_out, relb_out)[br], 16)
                            sp.wait_ge(biased, i * 16 + 8 * (4 * br + pp) + START)
                            if br == 0:
                                src = src_bias[ds(i * 4 + 2 * pp, 2), :].partition_broadcast(P)
                            else:
                                src = src_bias.rearrange("h p s -> p h s")[:, ds(i * 4 + 2 * pp, 2), :]
                            sp.dma_start(bias[:, :, :], src).then_inc(bias_in, 16)

        def sp_branch(sp, br):
            w = (branch_w_a, branch_w_b)[br]
            with sp.Fori(0, DT // 4) as i:
                for k in range(2):
                    sp_load(sp, U_BR[br], 2, i, k, tiles_of(w, ds(i * 4 * P + k * 2 * P, 2 * P), 4))

        def load_first_block(eng, b):
            for q in range(2):
                for m in range(2):
                    cols = slice(m * D + b * (AC // 2), m * D + (b + 1) * (AC // 2))
                    eng.dma_start(adas[:, b, 4 * q:4 * q + 4, m * (AC // 2):(m + 1) * (AC // 2)],
                                  ada_w.rearrange("a (p k) n -> p (a k) n", k=DT)[:, 4 * q:4 * q + 4, cols]
                                  ).then_inc(adas_in[b][q], 16)

        block = ctx.enter_context(nc.Block())

        @block.sync
        def _(sp):
            sp.dma_start(ccol[:, :], c.rearrange("a (p k) -> p (a k)", k=DT)).then_inc(c_in, 16)
            row = 0
            for src in (norm_ffn1, norm_mix, norm_ffn2, ada_b, branch_gate_b, final_norm.rearrange("(a n) -> a n", a=1)):
                n = src.shape[1] // P
                sp.dma_start(prm_in[row:row + n, :], src.rearrange("a (r n) -> (a r) n", n=P)).then_inc(prm_loaded, 16)
                row += n
            for t in range(TT):
                sp.dma_start(xin[:, t, :], x[0, t * P:(t + 1) * P, :]).then_inc(x_in[t], 16)
            sp.dma_start(fb[:, :], forget_b.rearrange("a h -> h a")).then_inc(fb_in, 16)
            load_first_block(sp, 1)
            for k in range(2):
                sp_load(sp, 0, 0, 0, k, tiles_of((ffn1_w_gate, ffn1_w_up)[k], slice(0, P)))
            load_first_block(sp, 2)
            load_first_block(sp, 3)
            sp_ffn(sp, ffn1_w_gate, ffn1_w_up, ffn1_w_down, U_GU1, U_DN1, True)
            sp_load(sp, U_FA, 0, 0, 0, tiles_of(mix_w_in, slice(OFF_F, OFF_F + P)))
            sp_pairs(sp, 0)
            sp_branch(sp, 0)
            sp_pairs(sp, 1)
            sp_branch(sp, 1)
            with sp.Fori(0, DT // 2) as i:
                for k in range(2):
                    sp_load(sp, U_OUT, 2, i, k, tiles_of(mix_w_out, ds(i * 2 * P + k * P, P)))
            sp_ffn(sp, ffn2_w_gate, ffn2_w_up, ffn2_w_down, U_GU2, U_DN2, False)
            for t in range(TT):
                for e in range(2):
                    sp.wait_ge(y_ready[e], t + 1)
                sp.dma_start(out[0, t * P:(t + 1) * P, :], y[:, t, :]).then_inc(out_sent, 16)
            sp.wait_ge(out_sent, 16 * TT)

        @block.gpsimd
        def _(pool):
            pool.wait_ge(consts_v, 5)
            nc.gpsimd.affine_select(out=ident[:, :], in_=ident[:, :], compare_op=ALU.not_equal, fill=1.0, base=0,
                                    pattern=[[-1, P]], channel_multiplier=1).then_inc(ident_made, 1)
            nc.gpsimd.affine_select(out=mask[0][:, :], in_=mask[0][:, :], compare_op=ALU.is_ge, fill=NEG_INF, base=0,
                                    pattern=[[-1, P]], channel_multiplier=1).then_inc(masks_made, 1)
            for n in range(4):
                pool.wait_ge(ms_done, n + 1)
                nc.gpsimd.tensor_tensor(nrm[:, 1, :], nrm[:, 0, :], mhalf[:, :], ALU.pow).then_inc(pow_done, 1)
                if n == 1:
                    pool.wait_ge(unit_done, U_FA)
                    pool.dma_start(rel[:, :], rel_bias[0, :, :]).then_inc(rel_in, 16)
                    pool.wait_ge(negF_done, 1)
                    pool.dma_start(negF_d, fgate[:, 5, :]).then_inc(negF_out, 16)
                    pool.wait_ge(relx_done, 2)
                    pool.dma_start(relx_d, relx[:, :]).then_inc(relx_out, 16)
                    pool.wait_ge(relx_out, 16)
                    pool.dma_start(relb_d, bass.AP(relx_d.tensor, P, [[SEQ + P, HB], [-1, P], [1, SEQ]])).then_inc(relb_out, 16)

        @block.scalar
        def _(act):
            def wait_apart(s, v):
                act.wait_ge(s, v)

            def prep(base, stride, i, k, n=UT):
                u = base + k
                if u >= U_END:
                    return
                s = u % 2
                act.wait_ge(raw_in[s], landed(base, stride, i, k))
                if u >= 2:
                    act.wait_ge(unit_done, u - 1 + i * stride)
                nc.scalar.activation(wH[s][:, :n * P], raw[s][:, :n * P], ACT.Copy).then_inc(hi_done, 1)

            def normed(n):
                for d in range(DT):
                    act.wait_ge(tmp_done, n * DT + d + 1)
                    nc.scalar.activation(hH[:, d, :], tmp[:, d % 2, :], ACT.Identity,
                                         bias=mod[:, M_SH[n] + d:M_SH[n] + d + 1]).then_inc(hH_done, 1)

            def gate_up(n, u0):
                with act.Fori(0, FT // 2) as i:
                    for k in range(4):
                        prep(u0, 4, i, k + 2)
                        j = k // 2
                        if k % 2 == 0:
                            act.wait_ge(prod_done[n][j], i + START)
                            act.wait_ge(unit_done, i * 4 + u0 + k + 1)
                            nc.scalar.activation(sg[:, j, :], bank[:, k, :], ACT.Silu).then_inc(silu_done[n][j], 1)
                        else:
                            wait_apart(prod_done[n][j], i + 1 + START)
                            nc.scalar.activation(actH[:, ds(i * 2 + j, 1), :], pr[:, j:j + 1, :], ACT.Copy).then_inc(actH_done[n], 1)

            def squares(m, j, i):
                act.wait_ge(ssqa_done[m], i * 2 + j + START)
                wait_apart(x_done[m][j], i + 1 + START)
                nc.scalar.activation(tmp[:, j:j + 1, :], xT[:, ds(i * 2 + j, 1), :], ACT.Square).then_inc(sq_done[m], 1)

            def down(n, m, u0):
                def body(i):
                    for k in range(6):
                        if not (isinstance(i, int) and n == 1 and k >= 4):
                            prep(u0, 6, i, k + 2, PARTS[(k + 2) % 3][1])
                        if k % 3 == 2:
                            squares(m, k // 3, i)
                            if n == 1:
                                t = ds(i * 2 + k // 3, 1)
                                nc.scalar.activation(xg[:, t, :], xT[:, t, :], ACT.Copy,
                                                     scale=prm[:, ds(i * 2 + (C_NF + k // 3), 1)]).then_inc(xg_done, 1)
                with act.Fori(0, DT // 2 - n) as i:
                    body(i)
                if n == 1:
                    body(DT // 2 - 1)

            def pairs(br):
                u0 = U_MIX[br]
                if br == 1:
                    act.wait_ge(y_done, DT + Y_START)
                with act.Fori(0, PAIRS // 2) as i:
                    for pp in range(2):
                        g = i * 2 + (4 * br + pp)
                        k0 = 5 * pp
                        for k, dst, sc in ((0, qH, SCALE), (1, kH, 1.0)):
                            prep(u0, 10, i, k0 + k + 2)
                            act.wait_ge(s_done, g * 8 + START)
                            act.wait_ge(unit_done, i * 10 + u0 + k0 + k + 1)
                            nc.scalar.activation(dst[:, :], bank[:, k, :], ACT.Copy, scale=sc).then_inc(qhi, 1)
                        prep(u0, 10, i, k0 + 4)
                        act.wait_ge(unit_done, i * 10 + u0 + k0 + 3)
                        nc.scalar.activation(vT[:, :], bank[:, 0, :], ACT.Copy).then_inc(v_copied, 1)
                        for h in range(2):
                            for n, t in enumerate(T_ORDER):
                                w = P * (t + 1)
                                act.wait_ge(biased, g * 8 + (4 * h + n + 1) + START)
                                nc.scalar.activation(prob[:, h, T_OFF[t]:T_OFF[t] + w], prob[:, h, T_OFF[t]:T_OFF[t] + w],
                                                     ACT.Exp, scale=-1.0, bias=negmax[:, h, t:t + 1],
                                                     accum_out=rowsum[:, h, t:t + 1]).then_inc(exp_done, 1)
                            if h == 0:
                                act.wait_ge(v_turned, g + 1)
                                nc.scalar.activation(vH[:, :, :], bank[:, 1, :].rearrange("p (a b) -> p a b", a=TT),
                                                     ACT.Copy).then_inc(vhi, 1)

                        def gate(n):
                            wait_apart(unit_done, i * 10 + u0 + k0 + 4 + n)
                            col = i * 4 + C_GB + br * DT + 2 * pp + n
                            nc.scalar.activation(gbuf[:, ds(i * 4 + 2 * pp + n, 1), :], bank[:, n:n + 1, :], ACT.Identity,
                                                 bias=prm[:, ds(col, 1)]).then_inc(d_free[n], 1)

                        def turned_hi(h):
                            act.wait_ge(pv_done, g * 2 + h + START)
                            for n, cols in enumerate(PIECE_COLS):
                                act.wait_ge(p_turned, g * 4 + (2 * h + n + 1))
                                sbk = S_BANK[h]
                                nc.scalar.activation(ptH[:, cols], bank[:, sbk:sbk + 3, :].rearrange("p a b -> p (a b)")[:, cols],
                                                     ACT.Copy).then_inc(pthi, 1)

                        def out_hi(h):
                            wait_apart(pv_done, g * 2 + h + 1 + START)
                            rows = slice(DH * h, DH * h + DH)
                            nc.scalar.activation(oH[rows, ds(i * 2 + pp, 1), :], bank[rows, S_BANK[h]:S_BANK[h] + 1, :],
                                                 ACT.Copy).then_inc(ohi[h], 1)

                        turned_hi(0)
                        prep(u0, 10, i, k0 + 5)
                        gate(0)
                        out_hi(0)
                        turned_hi(1)
                        prep(u0, 10, i, k0 + 6)
                        gate(1)
                        out_hi(1)

            def branch(br):
                act.wait_ge(d_free[0], 1 + 2 * PAIRS * (br + 1))
                act.wait_ge(d_free[1], 3 * PAIRS * (br + 1) + START)
                for d in range(DT):
                    nc.scalar.activation(gbuf[:, d, :], gbuf[:, d, :], ACT.Sigmoid).then_inc(gates_done, 1)
                with act.Fori(0, DT // 4) as i:
                    for k in range(2):
                        prep(U_BR[br], 2, i, k + 2)
                        if br == 1:
                            for e in range(2):
                                t = ds(i * 4 + 2 * k + e, 1)
                                wait_apart(yadd_done, i * 4 + (2 * k + e + 1))
                                nc.scalar.activation(hH[:, t, :], ymix[:, t, :], ACT.Copy).then_inc(yhi, 1)

            for first in silu_done[0] + silu_done[1]:
                act.sem_inc(first, START)
            load_first_block(act, 0)
            act.wait_ge(c_in, 16)
            nc.scalar.activation(csilu[:, :], ccol[:, :], ACT.Silu).then_inc(c_act, 1)
            act.wait_ge(prm_T, 1)
            nc.scalar.activation(prm[:, :N_PRM], bank[:, 0, :N_PRM], ACT.Copy).then_inc(prm_done, 1)
            for t in range(TT):
                act.wait_ge(x_in[t], 16)
                if t >= 1:
                    act.wait_ge(ssq_x, t)
                nc.scalar.activation(sqx[:, :], xin[:, t, :], ACT.Square, accum_out=ssq0[:, t:t + 1]).then_inc(ssq_x, 1)
            for d in range(DT):
                act.wait_ge(xt_psum, d + 1)
                nc.scalar.activation(xT[:, d, :], bank[:, 1 + d % 2, :], ACT.Copy).then_inc(xt_done, 1)
            for k in range(2):
                prep(0, 0, 0, k)
            normed(0)
            gate_up(0, U_GU1)
            down(0, 0, U_DN1)
            normed(1)
            prep(U_FA, 0, 0, 2)
            act.wait_ge(unit_done, U_FA + 1)
            nc.scalar.activation(fgate[:, 0, :], bank[0:HA, B_FA, :], ACT.Abs, bias=fb[:, :]).then_inc(fa_act, 1)
            nc.scalar.activation(fgate[:, 3, :], bank[0:HA, B_FA, :], ACT.Relu, bias=nfb[:, :], scale=-1.0).then_inc(d_free[0], 1)
            act.wait_ge(fa_act, 1)
            nc.scalar.activation(fgate[:, 1, :], fgate[:, 0, :], ACT.Exp, scale=-1.0).then_inc(fa_act, 1)
            act.wait_ge(fa_act, 2)
            nc.scalar.activation(fgate[:, 2, :], fgate[:, 1, :], ACT.Ln, bias=1.0).then_inc(fa_act, 1)
            act.wait_ge(fa_act, 3)
            nc.scalar.activation(fgate[:, 4, :], fgate[:, 2, :], ACT.Exp, scale=-1.0).then_inc(fa_act, 1)
            pairs(0)
            branch(0)
            pairs(1)
            branch(1)
            with act.Fori(0, DT // 2) as i:
                for k in range(2):
                    prep(U_OUT, 2, i, k + 2)
                    squares(1, k, i)
            normed(2)
            gate_up(1, U_GU2)
            down(1, 2, U_DN2)
            act.wait_ge(newton, 3 * 4)
            for t in range(TT):
                act.wait_ge(yt_done, 2 * t + 1)
                nc.scalar.activation(y[:, t, :SEQ], bank[:, Y_BANK[2 * t], :], ACT.Copy,
                                     scale=nrm[:, 4, t:t + 1]).then_inc(y_ready[0], 1)

        @block.vector
        def _(dve):
            V = nc.vector

            def wait_apart(s, v, at):
                dve.wait_ge(s, v)
                V.memset(at, 0.0)

            def prep(base, stride, i, k, n=UT):
                u = base + k
                if u >= U_END:
                    return
                s = u % 2
                dve.wait_ge(hi_done, u + 1 + i * stride)
                V.tensor_tensor(wL[s][:, :n * P], raw[s][:, :n * P], f32(wH[s][:, :n * P]), ALU.subtract).then_inc(lo_done, 1)

            def ada_rows(done, i, rows, width):
                for k in rows:
                    q, r = k // 4, k % 4
                    if r == 0:
                        dve.wait_ge(adaw_in[q], i * 16 + 16 * (done + 1))
                    if k == 0:
                        ins = V.tensor_scalar(adac[:, :width], adaw[:, q, r, :width], csilu[:, 0:1], None, ALU.mult)
                    else:
                        dve.wait_ge(ada_step, i * 8 + (8 * done + k))
                        ins = V.scalar_tensor_tensor(out=adac[:, :width], in0=adaw[:, q, r, :width], scalar=csilu[:, k:k + 1],
                                                     in1=adac[:, :width], op0=ALU.mult, op1=ALU.add)
                    ins.then_inc(ada_step, 1)
                    if r == 3:
                        dve.wait_ge(ada_step, i * 8 + (8 * done + 4 * q + 4))
                        dve.sem_inc(adaw_used[q], 1)

            def ada_mod(done, i, col, nt):
                dve.wait_ge(ada_sum, i + (done + 1))
                V.tensor_tensor(mod[:, ds(col, nt)], bank[:, B_ADA, 0:nt], prm[:, ds(col + C_AB, nt)], ALU.add).then_inc(mod_done, 1)

            def rstd(n):
                if n == 0:
                    dve.wait_ge(ssq_x, TT)
                    src = ssq0[:, :]
                else:
                    dve.wait_ge(ssq_ps, n)
                    src = bank[:, B_SSQ, 0:TT]
                V.tensor_scalar(nrm[:, 0, :], src, 1.0 / D, EPS, ALU.mult, ALU.add).then_inc(ms_done, 1)
                dve.wait_ge(pow_done, n + 1)
                V.scalar_tensor_tensor(out=nrm[:, 2, :], in0=nrm[:, 1, :], scalar=-0.5, in1=nrm[:, 1, :],
                                       op0=ALU.mult, op1=ALU.mult).then_inc(newton, 1)
                dve.wait_ge(newton, 3 * n + 1)
                V.tensor_tensor(nrm[:, 3, :], nrm[:, 2, :], nrm[:, 0, :], ALU.mult).then_inc(newton, 1)
                dve.wait_ge(newton, 3 * n + 2)
                V.scalar_tensor_tensor(out=nrm[:, 4, :], in0=nrm[:, 3, :], scalar=1.5, in1=nrm[:, 1, :],
                                       op0=ALU.add, op1=ALU.mult).then_inc(newton, 1)
                dve.wait_ge(newton, 3 * n + 3)

            def normed(n):
                rstd(n)
                V.tensor_tensor(diag[:, :, :], ident[:, :].rearrange("p (a b) -> p a b", a=1).to_broadcast([P, TT, P]),
                                nrm[:, 4, :].rearrange("p (a b) -> p a b", b=1).to_broadcast([P, TT, P]),
                                ALU.mult).then_inc(diag_done, 1)
                dve.wait_ge(bc_done, n + 1)
                if n == 0:
                    dve.wait_ge(xt_done, DT)
                else:
                    dve.wait_ge(gs_done, n)
                for b in range(DT // 2):
                    if n == 0:
                        if b >= 1 and b + 1 < ADA0:
                            first_rows(b + 1)
                        first_columns(b)
                    for d in (2 * b, 2 * b + 1):
                        if b >= 1:
                            dve.wait_ge(hL_done, n * DT + d - 1)
                        V.scalar_tensor_tensor(out=tmp[:, d % 2, :], in0=xT[:, d, :], scalar=gs[:, n, d:d + 1],
                                               in1=bank[:, B_BC, :], op0=ALU.mult, op1=ALU.mult).then_inc(tmp_done, 1)
                    for d in (2 * b, 2 * b + 1):
                        dve.wait_ge(hH_done, n * DT + d + 1)
                        V.scalar_tensor_tensor(out=hL[:, d, :], in0=tmp[:, d % 2, :], scalar=mod[:, M_SH[n] + d:M_SH[n] + d + 1],
                                               in1=f32(hH[:, d, :]), op0=ALU.add, op1=ALU.subtract).then_inc(hL_done, 1)

            def first_rows(b):
                for k in range(DT):
                    if k % 4 == 0:
                        dve.wait_ge(adas_in[b][k // 4], 32)
                    if k == 0:
                        ins = V.tensor_scalar(adasc[:, b, :], adas[:, b, 0, :], csilu[:, 0:1], None, ALU.mult)
                    else:
                        dve.wait_ge(adas_step, DT * b + k)
                        ins = V.scalar_tensor_tensor(out=adasc[:, b, :], in0=adas[:, b, k, :], scalar=csilu[:, k:k + 1],
                                                     in1=adasc[:, b, :], op0=ALU.mult, op1=ALU.add)
                    ins.then_inc(adas_step, 1)

            def first_columns(b):
                def pick(t, c0, stride):
                    return t[:, c0:c0 + 2 * stride].rearrange("p (a d) -> p a d", a=2)
                dve.wait_ge(adas_sum, b + 1)
                V.tensor_tensor(pick(mod, 0, DT)[:, :, 2 * b:2 * b + 2],
                                bank[:, B_ADA_START[b], 0:4].rearrange("p (a d) -> p a d", a=2),
                                pick(prm, C_AB, DT)[:, :, 2 * b:2 * b + 2], ALU.add).then_inc(mod_first, 1)
                dve.wait_ge(mod_first, 2 * b + 1)
                V.scalar_tensor_tensor(out=gs[:, 0, 2 * b:2 * b + 2], in0=mod[:, DT + 2 * b:DT + 2 * b + 2], scalar=1.0,
                                       in1=prm[:, C_N1 + 2 * b:C_N1 + 2 * b + 2], op0=ALU.add, op1=ALU.mult).then_inc(mod_first, 1)
                dve.wait_ge(mod_first, 2 * b + 2)
                if b == ADA0 - 2:
                    for q in range(2):
                        dve.sem_inc(adaw_used[q], START)

            def scale_columns(n, g_col):
                V.scalar_tensor_tensor(out=gs[:, n, :], in0=mod[:, M_SC[n]:M_SC[n] + DT], scalar=1.0,
                                       in1=prm[:, g_col:g_col + DT], op0=ALU.add, op1=ALU.mult).then_inc(gs_done, 1)

            def gate_up(n, u0, ada):
                with dve.Fori(0, FT // 2) as i:
                    for k in range(4):
                        j = k // 2
                        if k % 2:
                            dve.wait_ge(silu_done[n][j], i + 1 + START)
                            dve.wait_ge(unit_done, i * 4 + u0 + k + 1)
                            dve.wait_ge(actL_done[n], i * 2 + START)
                            V.tensor_tensor(pr[:, j, :], sg[:, j, :], bank[:, k, :], ALU.mult).then_inc(prod_done[n][j], 1)
                        prep(u0, 4, i, k + 2)
                        if k % 2:
                            dve.wait_ge(actH_done[n], i * 2 + j + 1)
                            V.tensor_tensor(actL[:, ds(i * 2 + j, 1), :], pr[:, j:j + 1, :], f32(actH[:, ds(i * 2 + j, 1), :]),
                                            ALU.subtract).then_inc(actL_done[n], 1)
                        if ada and k < 3:
                            ada_rows(0, i, (range(3), range(3, 5), range(5, 8))[k], AC)
                        if ada and k == 3:
                            ada_mod(0, i, i * (AC // P) + ADA0 * (AC // P), AC // P)

            def residual(m, j, i, b, u):
                dve.wait_ge(unit_done, u)
                V.scalar_tensor_tensor(out=xT[:, ds(i * 2 + j, 1), :], in0=bank[:, b:b + 1, :],
                                       scalar=gres[:, m, ds(i * 2 + j, 1)], in1=xT[:, ds(i * 2 + j, 1), :],
                                       op0=ALU.mult, op1=ALU.add).then_inc(x_done[m][j], 1)

            def add_squares(m, j, i):
                dve.wait_ge(sq_done[m], i * 2 + j + 1)
                dve.wait_ge(ssqa_done[m], i * 2 + j + START)
                V.tensor_tensor(ssqa[:, :], ssqa[:, :], tmp[:, j, :], ALU.add).then_inc(ssqa_done[m], 1)

            def down(n, m, u0, ada):
                def body(i):
                    for k in range(6):
                        if k % 3 == 2:
                            residual(m, k // 3, i, 5 + k // 3, i * 6 + u0 + k + 1)
                        if not (isinstance(i, int) and n == 1 and k >= 4):
                            prep(u0, 6, i, k + 2, PARTS[(k + 2) % 3][1])
                        if k % 3 == 2:
                            add_squares(m, k // 3, i)
                        if ada and k in (1, 3):
                            ada_rows(ADA1, i, range(4 * (k // 2), 4 * (k // 2) + 4), AC2)
                        if ada and k == 5:
                            ada_mod(ADA1, i, i * (AC2 // P) + (ADA0 + ADA1) * (AC // P), AC2 // P)
                with dve.Fori(0, DT // 2 - n) as i:
                    body(i)
                if n == 1:
                    body(DT // 2 - 1)

            def pairs(br):
                u0 = U_MIX[br]
                with dve.Fori(0, PAIRS // 2) as i:
                    for pp in range(2):
                        g = i * 2 + (4 * br + pp)
                        k0 = 5 * pp
                        dve.wait_ge(qhi, g * 2 + 1)
                        V.scalar_tensor_tensor(out=qL[:, :], in0=bank[:, 0, :], scalar=SCALE, in1=f32(qH[:, :]),
                                               op0=ALU.mult, op1=ALU.subtract).then_inc(d_free[0], 1)
                        prep(u0, 10, i, k0 + 2)
                        dve.wait_ge(qhi, g * 2 + 2)
                        V.tensor_tensor(kL[:, :], bank[:, 1, :], f32(kH[:, :]), ALU.subtract).then_inc(d_free[1], 1)
                        prep(u0, 10, i, k0 + 3)
                        prep(u0, 10, i, k0 + 4)

                        def biased_scores(h):
                            for n, t in enumerate(T_ORDER):
                                w = P * (t + 1)
                                b0 = (0, SEQ - w)[br]
                                if n == 0:
                                    dve.wait_ge(bias_in, g * 16 + 16)
                                wait_apart(s_done, g * 8 + (4 * h + (1, 3, 3, 4)[n]) + START, spare[:, 4 * h + n:4 * h + n + 1])
                                V.tensor_tensor_reduce(
                                    out=prob[:, h, T_OFF[t]:T_OFF[t] + w],
                                    in0=bank[:, S_BANK[h]:S_BANK[h] + 3, :].rearrange("p a b -> p (a b)")[:, T_OFF[t]:T_OFF[t] + w],
                                    in1=bias[:, h, b0:b0 + w], scale=-1.0, scalar=BIG, op0=ALU.add, op1=ALU.min,
                                    accum_out=negmax[:, h, t:t + 1]).then_inc(biased, 1)

                        def normalised(h):
                            dve.wait_ge(exp_done, g * 8 + (4 * h + 4))
                            V.reciprocal(rinv[:, h, :], rowsum[:, h, :]).then_inc(rinv_done, 1)
                            dve.wait_ge(rinv_done, g * 2 + h + 1)
                            for n, t in enumerate(T_ORDER):
                                a = prob[:, h, T_OFF[t]:T_OFF[t] + P * (t + 1)]
                                V.tensor_scalar(a, a, rinv[:, h, t:t + 1], None, ALU.mult).then_inc(p_ready, 1)

                        def turned_lo(h):
                            for n, cols in enumerate(PIECE_COLS):
                                dve.wait_ge(pthi, g * 4 + (2 * h + n + 1))
                                V.tensor_tensor(ptL[:, cols], bank[:, S_BANK[h]:S_BANK[h] + 3, :].rearrange("p a b -> p (a b)")[:, cols],
                                                f32(ptH[:, cols]), ALU.subtract).then_inc(pt_ready, 1)

                        def out_lo(h):
                            rows = slice(DH * h, DH * h + DH)
                            dve.wait_ge(ohi[h], g + 1)
                            V.tensor_tensor(oL[rows, ds(i * 2 + pp, 1), :], bank[rows, S_BANK[h]:S_BANK[h] + 1, :],
                                            f32(oH[rows, ds(i * 2 + pp, 1), :]), ALU.subtract).then_inc(o_ready[h], 1)

                        biased_scores(0)
                        biased_scores(1)
                        normalised(0)
                        dve.wait_ge(vhi, g + 1)
                        V.tensor_tensor(vL[:, :, :], bank[:, 1, :].rearrange("p (a b) -> p a b", a=TT), f32(vH[:, :, :]),
                                        ALU.subtract).then_inc(d_free[1], 1)
                        normalised(1)
                        turned_lo(0)
                        prep(u0, 10, i, k0 + 5)
                        out_lo(0)
                        turned_lo(1)
                        prep(u0, 10, i, k0 + 6)
                        out_lo(1)

            def branch(br):
                u0 = U_BR[br]
                with dve.Fori(0, DT // 4) as i:
                    for k in range(2):
                        dve.wait_ge(unit_done, i * 2 + u0 + k + 1)
                        for e in range(2):
                            t = ds(i * 4 + 2 * k + e, 1)
                            dve.wait_ge(gates_done, i * 4 + (DT * br + 2 * k + e + 1))
                            if br == 0:
                                V.tensor_tensor(ymix[:, t, :], bank[:, 2 + 2 * k + e:3 + 2 * k + e, :], gbuf[:, t, :],
                                                ALU.mult).then_inc(y_done, 1)
                            else:
                                V.tensor_tensor(gbuf[:, t, :], bank[:, 2 + 2 * k + e:3 + 2 * k + e, :], gbuf[:, t, :],
                                                ALU.mult).then_inc(y_done, 1)
                        if br == 1:
                            for e in range(2):
                                t = ds(i * 4 + 2 * k + e, 1)
                                dve.wait_ge(y_done, i * 4 + DT + 2 * k + e + 1 + Y_START)
                                V.tensor_tensor(ymix[:, t, :], ymix[:, t, :], gbuf[:, t, :], ALU.add).then_inc(yadd_done, 1)
                        prep(u0, 2, i, k + 2)
                        if br == 1:
                            for e in range(2):
                                t = ds(i * 4 + 2 * k + e, 1)
                                dve.wait_ge(yhi, i * 4 + (2 * k + e + 1))
                                V.tensor_tensor(hL[:, t, :], ymix[:, t, :], f32(hH[:, t, :]), ALU.subtract).then_inc(yH_ready, 1)

            dve.sem_inc(lo_done, FREE)
            for first in (prod_done[0] + prod_done[1] + [mod_done] + x_done[0] + x_done[1] + x_done[2]
                          + actL_done + ssqa_done + [biased, d_free[1]] + o_ready):
                dve.sem_inc(first, START)
            dve.sem_inc(y_done, Y_START)
            V.memset(ident[:, :], 0.0).then_inc(consts_v, 1)
            V.memset(mask[0][:, :], 0.0).then_inc(consts_v, 1)
            V.memset(mask[1][:, :], 0.0).then_inc(consts_v, 1)
            V.memset(ones[:, :], 1.0).then_inc(consts_v, 1)
            V.memset(mhalf[:, :], -0.5).then_inc(consts_v, 1)
            dve.wait_ge(consts_v, 3)
            V.memset(mask[1][0:64, 64:P], NEG_INF).then_inc(masks_made, 1)
            dve.wait_ge(ident_made, 1)
            V.tensor_copy(identb[:, :], ident[:, :]).then_inc(identb_made, 1)
            dve.wait_ge(c_act, 1)
            first_rows(0)
            first_rows(1)
            dve.wait_ge(fb_in, 16)
            V.tensor_scalar(nfb[:, :], fb[:, :], -1.0, None, ALU.mult).then_inc(fa_sem, 1)
            dve.wait_ge(prm_done, 1)
            for k in range(2):
                prep(0, 0, 0, k)
            normed(0)
            gate_up(0, U_GU1, True)
            dve.wait_ge(mod_done, ADA1 + START)
            V.tensor_scalar(gres[:, 0, :], mod[:, M_G[0]:M_G[0] + DT], 0.5, None, ALU.mult).then_inc(cols_done, 1)
            scale_columns(1, C_NM)
            V.tensor_copy(gres[:, 1, :], mod[:, M_G[1]:M_G[1] + DT]).then_inc(cols_done, 1)
            V.memset(ssqa[:, :], 0.0).then_inc(cols_done, 1)
            dve.wait_ge(cols_done, 3)
            down(0, 0, U_DN1, True)
            dve.wait_ge(mod_done, ADA1 + ADA2 + START)
            scale_columns(2, C_N2)
            V.tensor_scalar(gres[:, 2, :], mod[:, M_G[2]:M_G[2] + DT], 0.5, None, ALU.mult).then_inc(cols_done, 1)
            normed(1)
            prep(U_FA, 0, 0, 2)
            z = fgate
            dve.wait_ge(fa_act, 2)
            V.tensor_scalar(z[:, 0, :], z[:, 1, :], 1.0, -1.0, ALU.add, ALU.add).then_inc(fa_sem, 1)
            dve.wait_ge(fa_sem, 2)
            V.tensor_tensor(z[:, 5, :], z[:, 1, :], z[:, 0, :], ALU.subtract).then_inc(fa_sem, 1)
            dve.wait_ge(fa_act, 3)
            dve.wait_ge(d_free[0], 1)
            dve.wait_ge(fa_sem, 3)
            V.tensor_tensor(z[:, 0, :], z[:, 2, :], z[:, 3, :], ALU.add).then_inc(fa_sem, 1)
            dve.wait_ge(fa_act, 4)
            V.tensor_tensor(z[:, 5, :], z[:, 5, :], z[:, 4, :], ALU.mult).then_inc(fa_sem, 1)
            dve.wait_ge(fa_sem, 5)
            V.tensor_tensor(z[:, 0, :], z[:, 0, :], z[:, 5, :], ALU.add).then_inc(fa_sem, 1)
            dve.wait_ge(fa_sem, 6)
            V.tensor_tensor_scan(z[:, 5, :], ones[0:HA, 0:1].to_broadcast([HA, SEQ]), z[:, 0, :], 0.0,
                                 ALU.mult, ALU.add).then_inc(negF_done, 1)
            pairs(0)
            dve.wait_ge(rel_in, 16)
            half = SEQ + P - (N_REL - 1)
            V.tensor_copy(relx[:, :half], rel[:, N_REL - 1:N_REL].to_broadcast([HB, half])).then_inc(relx_done, 1)
            V.tensor_copy(relx[:, half:], rel[:, N_REL - 1:0:-1]).then_inc(relx_done, 1)
            V.memset(ssqa[:, :], 0.0).then_inc(cols_done, 1)
            branch(0)
            pairs(1)
            branch(1)
            with dve.Fori(0, DT // 2) as i:
                for k in range(2):
                    residual(1, k, i, 2 + k, i * 2 + U_OUT + k + 1)
                    prep(U_OUT, 2, i, k + 2)
                    add_squares(1, k, i)
            normed(2)
            gate_up(1, U_GU2, False)
            V.memset(ssqa[:, :], 0.0).then_inc(cols_done, 1)
            dve.wait_ge(cols_done, 6)
            down(1, 2, U_DN2, False)
            rstd(3)
            for t in range(TT):
                dve.wait_ge(yt_done, 2 * t + 2)
                V.tensor_scalar(y[:, t, SEQ:], bank[:, Y_BANK[2 * t + 1], :], nrm[:, 4, t:t + 1], None,
                                ALU.mult).then_inc(y_ready[1], 1)

        @block.tensor
        def _(pe):
            T = nc.tensor

            def three(o, a, b, start, stop):
                T.matmul(o, a[0], b[0], start=start, stop=False)
                T.matmul(o, a[0], b[1], start=False, stop=False)
                return T.matmul(o, a[1], b[0], start=False, stop=stop)

            def tile(s, k):
                return wH[s][:, k * P:(k + 1) * P], wL[s][:, k * P:(k + 1) * P]

            def dense(u, s, o, rhs, ks, first, last, at=0):
                if at == 0:
                    pe.wait_ge(lo_done, u + 1 + FREE)
                for n, k in enumerate(ks):
                    ins = three(o, tile(s, at + n), (rhs[0][:, k, :], rhs[1][:, k, :]), first and n == 0,
                                last and n == len(ks) - 1)
                return ins

            h = (hH, hL)
            a = (actH, actL)
            o_ = (oH, oL)

            def h_unit(u, s, o, ks=range(DT)):
                return dense(u, s, o, h, ks, ks[0] == 0, ks[-1] == DT - 1, ks[0])

            def first_sums(b):
                pe.wait_ge(adas_step, DT * (b + 1))
                for n in range(AC // P):
                    ins = T.matmul(bank[:, B_ADA_START[b], n:n + 1], adasc[:, b, n * P:(n + 1) * P], ones[:, 0:1],
                                   start=True, stop=True)
                ins.then_inc(adas_sum, 1)

            def two_units(u, banks, ready):
                LAG = 3
                for k in range(DT + LAG):
                    if ready == 0 and k in (2, 4):
                        first_sums(k // 2 + 1)
                    for n in range(2):
                        t = k - n * LAG
                        if 0 <= t < DT:
                            if t == 0:
                                pe.wait_ge(lo_done, u + n + 1 + FREE)
                            if n == 0:
                                pe.wait_ge(hL_done, ready + t + 1)
                            ins = three(bank[:, banks[n], :], tile((u + n) % 2, t), (hH[:, t, :], hL[:, t, :]), t == 0, t == DT - 1)
                            if t == DT - 1:
                                ins.then_inc(unit_done, 1)

            def ada_sums(done, i, nt):
                pe.wait_ge(ada_step, i * 8 + 8 * (done + 1))
                pe.wait_ge(mod_done, i + done + START)
                for n in range(nt):
                    ins = T.matmul(bank[:, B_ADA, n:n + 1], adac[:, n * P:(n + 1) * P], ones[:, 0:1], start=True, stop=True)
                ins.then_inc(ada_sum, 1)

            def token_squares(m):
                pe.wait_ge(ssqa_done[m], DT + START)
                for t in range(TT):
                    ins = T.matmul(bank[:, B_SSQ, t:t + 1], ssqa[:, t * P:(t + 1) * P], ones[:, 0:1], start=True, stop=True)
                ins.then_inc(ssq_ps, 1)

            def spread(n):
                pe.wait_ge(diag_done, n + 1)
                for t in range(TT):
                    ins = T.matmul(bank[:, B_BC, t * P:(t + 1) * P], ones[:, :], diag[:, t, :], start=True, stop=True)
                ins.then_inc(bc_done, 1)

            def gate_up(n, u0, ready, ada):
                def body(i, k0):
                    for k in range(k0, 4):
                        pe.wait_ge((silu_done, prod_done)[k % 2][n][k // 2], i + START)
                        h_unit(i * 4 + u0 + k, (u0 + k) % 2, bank[:, k, :]).then_inc(unit_done, 1)
                    if ada:
                        ada_sums(0, i, AC // P)

                two_units(u0, (0, 1), ready)
                body(0, 2)
                with pe.Fori(1, FT // 2) as i:
                    body(i, 0)

            def down(n, m, u0, ada):
                with pe.Fori(0, DT // 2) as i:
                    for k in range(6):
                        k0, cnt = PARTS[k % 3]
                        j = k // 3
                        if k % 3 == 0:
                            pe.wait_ge(x_done[m][j], i + START)
                        pe.wait_ge(actL_done[n], k0 + cnt + START)
                        u = i * 6 + u0 + k
                        pe.wait_ge(lo_done, u + 1 + FREE)
                        for q in range(cnt):
                            f = k0 + q
                            ins = three(bank[:, 5 + j, :], tile((u0 + k) % 2, q), (actH[:, f, :], actL[:, f, :]),
                                        f == 0, f == FT - 1)
                        ins.then_inc(unit_done, 1)
                    if ada:
                        ada_sums(ADA1, i, AC2 // P)

            def pairs(br):
                u0 = U_MIX[br]
                if br == 1:
                    pe.wait_ge(y_done, DT + Y_START)
                def body(i, q_made=False):
                    for pp in range(2):
                        g = i * 2 + (4 * br + pp)
                        k0 = 5 * pp

                        def unit(k, b, ks=range(DT)):
                            return h_unit(i * 10 + u0 + k0 + k, (u0 + k0 + k) % 2, bank[:, b, :], ks)

                        def flat(hh):
                            return bank[:, S_BANK[hh]:S_BANK[hh] + 3, :].rearrange("p a b -> p (a b)")

                        def scores(hh):
                            rows = slice(DH * hh, DH * hh + DH)
                            pe.wait_ge(o_ready[hh], g + START)
                            for t in T_ORDER:
                                w = P * (t + 1)
                                o = flat(hh)[:, T_OFF[t]:T_OFF[t] + w]
                                three(o, (qH[rows, t * P:(t + 1) * P], qL[rows, t * P:(t + 1) * P]),
                                      (kH[rows, :w], kL[rows, :w]), True, False)
                                T.matmul(o[:, w - P:w], identb[:, :], mask[br][:, :], start=False, stop=True).then_inc(s_done, 1)

                        def turn(hh):
                            pe.wait_ge(p_ready, g * 8 + (4 * hh + 4))
                            for piece in J_PIECES:
                                for j in piece:
                                    for t in range(j, TT):
                                        ins = T.transpose(flat(hh)[:, J_OFF[j] + (t - j) * P:J_OFF[j] + (t - j + 1) * P],
                                                          prob[:, hh, T_OFF[t] + j * P:T_OFF[t] + (j + 1) * P], ident[:, :])
                                ins.then_inc(p_turned, 1)

                        def values(hh):
                            pe.wait_ge(d_free[1], g * 3 + 2 + START)
                            for j in range(TT):
                                if j < 2:
                                    pe.wait_ge(pt_ready, g * 4 + (2 * hh + j + 1))
                                w = SEQ - j * P
                                o = bank[:, S_BANK[hh], j * P:SEQ]
                                ins = three(o, (vH[:, j, :], vL[:, j, :]),
                                            (ptH[:, J_OFF[j]:J_OFF[j] + w], ptL[:, J_OFF[j]:J_OFF[j] + w]), j == 0, j == TT - 1)
                            ins.then_inc(pv_done, 1)

                        if not (q_made and pp == 0):
                            pe.wait_ge(d_free[0], g * 2 + 1)
                            unit(0, 0).then_inc(unit_done, 1)
                        pe.wait_ge(d_free[1], g * 3 + START)
                        unit(1, 1).then_inc(unit_done, 1)
                        pe.wait_ge(d_free[0], g * 2 + 2)
                        unit(2, 0).then_inc(unit_done, 1)
                        pe.wait_ge(d_free[1], g * 3 + 1 + START)
                        scores(0)
                        scores(1)
                        pe.wait_ge(v_copied, g + 1)
                        for t in range(TT):
                            ins = T.transpose(bank[:, 1, t * P:(t + 1) * P], vT[:, t * P:(t + 1) * P], ident[:, :])
                        ins.then_inc(v_turned, 1)
                        unit(3, 0).then_inc(unit_done, 1)
                        turn(0)
                        pe.wait_ge(d_free[1], g * 3 + 2 + START)
                        unit(4, 1, range(0, DT // 2))
                        values(0)
                        turn(1)
                        unit(4, 1, range(DT // 2, DT)).then_inc(unit_done, 1)
                        values(1)

                if br == 0:
                    body(0, True)
                with pe.Fori(1 - br, PAIRS // 2) as i:
                    body(i)

            def branch(br):
                u0 = U_BR[br]
                for hh in range(2):
                    pe.wait_ge(o_ready[hh], PAIRS * (br + 1) - hh + START)
                with pe.Fori(0, DT // 4) as i:
                    for k in range(2):
                        s = (u0 + k) % 2
                        pe.wait_ge(y_done, i * 4 + (br * DT - 2 + 2 * k) + Y_START)
                        pe.wait_ge(lo_done, i * 2 + u0 + k + 1 + FREE)
                        for e in range(2):
                            for q in range(PAIRS):
                                if k == e == 0 and q == PAIRS - 1:
                                    pe.wait_ge(o_ready[1], PAIRS * (br + 1) + START)
                                cols = slice((q * 2 + e) * P, (q * 2 + e + 1) * P)
                                ins = three(bank[:, 2 + 2 * k + e, :], (wH[s][:, cols], wL[s][:, cols]),
                                            (oH[:, q, :], oL[:, q, :]), q == 0, q == PAIRS - 1)
                        ins.then_inc(unit_done, 1)

            for first in (s_done, pv_done):
                pe.sem_inc(first, START)
            pe.wait_ge(ident_made, 1)
            pe.wait_ge(prm_loaded, 16 * 6)
            T.transpose(bank[:, 0, :N_PRM], prm_in[:N_PRM, :], ident[:N_PRM, :N_PRM]).then_inc(prm_T, 1)
            for t in range(TT):
                pe.wait_ge(x_in[t], 16)
            for d in range(DT):
                if d >= 2:
                    pe.wait_ge(xt_done, d - 1)
                for t in range(TT):
                    ins = T.transpose(bank[:, 1 + d % 2, t * P:(t + 1) * P], xin[:, t, d * P:(d + 1) * P], ident[:, :])
                ins.then_inc(xt_psum, 1)
            for b in range(2):
                first_sums(b)
            spread(0)
            gate_up(0, U_GU1, 0, True)
            down(0, 0, U_DN1, True)
            token_squares(0)
            spread(1)
            two_units(U_FA, (B_FA, 0), DT)
            pe.wait_ge(identb_made, 1)
            pe.wait_ge(masks_made, 2)
            pairs(0)
            branch(0)
            pairs(1)
            branch(1)
            with pe.Fori(0, DT // 2) as i:
                for k in range(2):
                    pe.wait_ge(x_done[1][k], i + START)
                    if k == 0:
                        pe.wait_ge(y_done, 2 * DT + Y_START)
                        pe.wait_ge(lo_done, i * 2 + U_OUT + k + 1 + FREE)
                        for q in range(DT):
                            pe.wait_ge(yH_ready, q + 1)
                            ins = three(bank[:, 2 + k, :], tile((U_OUT + k) % 2, q), (hH[:, q, :], hL[:, q, :]),
                                        q == 0, q == DT - 1)
                    else:
                        ins = h_unit(i * 2 + U_OUT + k, (U_OUT + k) % 2, bank[:, 2 + k, :])
                    ins.then_inc(unit_done, 1)
            token_squares(1)
            spread(2)
            gate_up(1, U_GU2, 2 * DT, False)
            down(1, 2, U_DN2, False)
            token_squares(2)
            pe.wait_ge(xg_done, DT)
            for t in range(TT):
                for e in range(2):
                    n = 2 * t + e
                    if n >= 6:
                        pe.wait_ge(y_ready[e], 1)
                    for q in range(4):
                        ins = T.transpose(bank[:, Y_BANK[n], q * P:(q + 1) * P], xg[:, 4 * e + q, t * P:(t + 1) * P], ident[:, :])
                    ins.then_inc(yt_done, 1)


_INS = ['x', 'c', 'ada_w', 'ada_b', 'norm_ffn1', 'ffn1_w_gate', 'ffn1_w_up', 'ffn1_w_down', 'norm_mix', 'mix_w_in',
        'forget_b', 'branch_gate_b', 'rel_bias', 'branch_w_a', 'branch_w_b', 'mix_w_out', 'norm_ffn2', 'ffn2_w_gate',
        'ffn2_w_up', 'ffn2_w_down', 'final_norm']
_OUTS = [((1, 512, 1024), 'float32')]


def kernel(**inputs):
    import numpy as _np
    import concourse.bacc as _bacc
    from concourse import mybir as _mybir
    from concourse.bass_utils import run_bass_kernel_spmd as _run

    nc = _bacc.Bacc("TRN2", target_bir_lowering=False, num_devices=1)
    arrays, args = {}, []
    for name in _INS:
        a = _np.ascontiguousarray(inputs[name])
        arrays[f"in_{name}_dram"] = a
        args.append(nc.dram_tensor(f"in_{name}_dram", a.shape, _mybir.dt.from_np(a.dtype), kind="ExternalInput").ap())
    for i, (shape, dtype) in enumerate(_OUTS):
        dt = _mybir.dt.from_np(_np.dtype(dtype))
        args.append(nc.dram_tensor(f"out_{i}_dram", shape, dt, kind="ExternalOutput").ap())
    hybrid_block(nc, *args)
    r = _run(nc, [arrays], core_ids=[0])
    return r.results[0]["out_0_dram"]
```

```python
from contextlib import ExitStack

import concourse.bass as bass
from concourse import mybir

ALU = mybir.AluOpType
ACT = mybir.ActivationFunctionType
F32 = mybir.dt.float32
F32R = mybir.dt.float32r
BF16 = mybir.dt.bfloat16
ds = bass.ds

P = 128
EPS = 1e-6
NEG_INF = -1e30
BIG = 3.0e38


def hybrid_block(nc, x, c, ada_w, ada_b, norm_ffn1, ffn1_w_gate, ffn1_w_up, ffn1_w_down,
                 norm_mix, mix_w_in, forget_b, branch_gate_b, rel_bias, branch_w_a, branch_w_b,
                 mix_w_out, norm_ffn2, ffn2_w_gate, ffn2_w_up, ffn2_w_down, final_norm, out):
    _, SEQ, D = x.shape
    DT = D // P
    TT = SEQ // P
    FF = ffn1_w_gate.shape[2]
    FT = FF // P
    HA = forget_b.shape[1]
    HB, N_REL = rel_bias.shape[1:]
    DH = 64
    WA, WB = HA * DH, HB * DH
    PAIRS = WA // P
    REL_CLIP = (N_REL - 1) // 2
    SCALE = DH ** -0.5
    N_MOD = ada_b.shape[1] // D
    UT = 8
    FREE = 2
    START = 1
    Y_START = START + 2
    assert SEQ == 512 and DT == 8 and FT == 22 and WA == WB == 512 and REL_CLIP == 128

    PARTS = [(0, 8), (8, 8), (16, 6)]
    U_GU1 = 0
    U_DN1 = U_GU1 + 2 * FT
    U_FA = U_DN1 + 3 * DT
    U_MIX = [U_FA + 1, 0]
    U_BR = [U_MIX[0] + 5 * PAIRS, 0]
    U_MIX[1] = U_BR[0] + DT // 2
    U_BR[1] = U_MIX[1] + 5 * PAIRS
    U_OUT = U_BR[1] + DT // 2
    U_GU2 = U_OUT + DT
    U_DN2 = U_GU2 + 2 * FT
    U_END = U_DN2 + 3 * DT

    OFF_A = (0, WA, 2 * WA)
    OFF_F = 3 * WA
    OFF_B = (3 * WA + HA, 3 * WA + HA + WB, 3 * WA + HA + 2 * WB)
    OFF_G = 3 * WA + HA + 3 * WB
    QKV_OFF = (OFF_A, OFF_B)

    T_ORDER = (3, 2, 0, 1)
    T_OFF = {3: 0, 2: 512, 0: 896, 1: 1024}
    J_PIECES = ((0,), (1, 3, 2))
    PIECE_COLS = (slice(0, 512), slice(512, 1280))
    J_OFF = {0: 0, 1: 512, 3: 896, 2: 1024}
    CW = 1280

    C_N1, C_NM, C_N2, C_AB, C_GB = 0, DT, 2 * DT, 3 * DT, 3 * DT + N_MOD * DT
    C_NF = C_GB + 2 * DT
    N_PRM = C_NF + DT
    M_SH = (0, 3 * DT, 6 * DT)
    M_SC = (DT, 4 * DT, 7 * DT)
    M_G = (2 * DT, 5 * DT, 8 * DT)

    ADA0, ADA1, ADA2 = 4, FT // 2, DT // 2
    AC, AC2 = 512, 384
    ROWS_V = (5, 5, 6, 6)
    N_LAST = ADA2 * AC2 // P
    assert (ADA0 + ADA1) * AC + ADA2 * AC2 == N_MOD * D

    ctx = ExitStack()
    with ctx:
        def sb(name, shape, dt=F32, stack=ctx):
            return stack.enter_context(nc.sbuf_tensor(name, shape, dt))

        def sem(name):
            return ctx.enter_context(nc.semaphore(name))

        xT = sb("xT", [P, DT, SEQ])
        hH = sb("hH", [P, DT, SEQ], F32R)
        hL = sb("hL", [P, DT, SEQ], F32R)
        raw = [sb(f"raw{s}", [P, UT * P]) for s in range(2)]
        wH = [sb(f"wH{s}", [P, UT * P], F32R) for s in range(2)]
        wL = [sb(f"wL{s}", [P, UT * P], F32R) for s in range(2)]
        ident = sb("ident", [P, P])
        identb = sb("identb", [P, P], BF16)
        mask = [sb(f"mask{b}", [P, P], BF16) for b in range(2)]
        ones = sb("ones", [P, P])
        onesr = sb("onesr", [P, 2], F32R)
        mhalf = sb("mhalf", [P, TT])
        prm_in = sb("prm_in", [P, P])
        prm = sb("prm", [P, P])
        mod = sb("mod", [P, N_MOD * DT])
        gs = sb("gs", [P, 3, DT])
        gres = sb("gres", [P, 3, DT])
        ccol = sb("ccol", [P, DT])
        csilu = sb("csilu", [P, DT])
        fb = sb("fb", [HA, 1])
        nfb = sb("nfb", [HA, 1])
        ssq0 = sb("ssq0", [P, TT])
        nrm = sb("nrm", [P, 5, TT])
        tmp = sb("tmp", [P, 2, SEQ])
        ssqa = sb("ssqa", [P, SEQ])
        diag = sb("diag", [P, TT, P])

        at_start = ExitStack()
        with at_start:
            xin = sb("xin", [P, TT, D], stack=at_start)
            sqx = sb("sqx", [P, D], stack=at_start)
            adas = sb("adas", [P, ADA0, DT, AC], stack=at_start)
            adasc = sb("adasc", [P, ADA0, AC], stack=at_start)
        in_ffn = ExitStack()
        with in_ffn:
            actH = sb("actH", [P, FT, SEQ], F32R, stack=in_ffn)
            actL = sb("actL", [P, FT, SEQ], F32R, stack=in_ffn)
            sg = sb("sg", [P, 2, SEQ], stack=in_ffn)
            pr = sb("pr", [P, 2, SEQ], stack=in_ffn)
            adaw = sb("adaw", [P, 2, DT // 2, AC], stack=in_ffn)
            adac = sb("adac", [P, AC], stack=in_ffn)
            adacH = sb("adacH", [P, AC], F32R, stack=in_ffn)
            adacL = sb("adacL", [P, AC], F32R, stack=in_ffn)
            adac2 = sb("adac2", [P, ADA2, AC2], stack=in_ffn)
        in_mix = ExitStack()
        with in_mix:
            gbuf = sb("gbuf", [P, DT, SEQ], stack=in_mix)
            oH = sb("oH", [P, PAIRS, SEQ], F32R, stack=in_mix)
            oL = sb("oL", [P, PAIRS, SEQ], F32R, stack=in_mix)
            ymix = sb("ymix", [P, DT, SEQ], stack=in_mix)
            prob = sb("prob", [P, 2, CW], stack=in_mix)
            ptH = sb("ptH", [P, CW], F32R, stack=in_mix)
            ptL = sb("ptL", [P, CW], F32R, stack=in_mix)
            qHH = sb("qHH", [P, 2, SEQ], F32R, stack=in_mix)
            kHL = sb("kHL", [P, 2, SEQ], F32R, stack=in_mix)
            qL = sb("qL", [P, SEQ], F32R, stack=in_mix)
            vT = sb("vT", [P, SEQ], stack=in_mix)
            vHL = sb("vHL", [P, 2, TT, P], F32R, stack=in_mix)
            osum = sb("osum", [P, SEQ], stack=in_mix)
            bias = sb("bias", [P, 2, SEQ], stack=in_mix)
            negmax = sb("negmax", [P, 2, TT], stack=in_mix)
            spare = sb("spare", [P, 2 * TT], stack=in_mix)
            rowsum = sb("rowsum", [P, 2, TT], stack=in_mix)
            rinv = sb("rinv", [P, 2, TT], stack=in_mix)
            fgate = sb("fgate", [HA, 6, SEQ], stack=in_mix)
            rel = sb("rel", [HB, N_REL], stack=in_mix)
            relx = sb("relx", [HB, SEQ + P], stack=in_mix)
        modrow = tmp[0:1, 0, :]
        modrows = prm_in[0:ADA1 * AC // P, :]
        xg = adaw[:, :, :, :].rearrange("p a b n -> p (a b) n")
        at_end = ExitStack()
        with at_end:
            y = sb("y", [P, TT, D], stack=at_end)

        bank = ctx.enter_context(nc.psum_tensor("bank", [P, 8, SEQ], F32))
        B_ADA, B_BC, B_SSQ, B_FA = 4, 4, 7, 7
        B_LAST = 5
        B_ADA_START = (3, 5, 6, 7)
        Y_BANK = ((0, 1, 2, 3), (4, 5, 6, 0))
        S_BANK = (2, 5)

        mod_d = nc.dram_tensor("mod_d", [1, ADA1 * AC], F32, kind="Internal").ap()
        negF_d = nc.dram_tensor("negF_d", [HA, SEQ], F32, kind="Internal").ap()
        relx_d = nc.dram_tensor("relx_d", [HB, SEQ + P], F32, kind="Internal").ap()
        relb_d = nc.dram_tensor("relb_d", [HB, P, SEQ], F32, kind="Internal").ap()

        raw_in = [sem(f"raw_in{s}") for s in range(2)]
        hi_done = sem("hi_done")
        lo_done = sem("lo_done")
        unit_done = sem("unit_done")
        c_in = sem("c_in")
        x_in = [sem(f"x_in{t}") for t in range(TT)]
        prm_loaded = sem("prm_loaded")
        fb_in = sem("fb_in")
        consts_v = sem("consts_v")
        ident_made = sem("ident_made")
        masks_made = sem("masks_made")
        identb_made = sem("identb_made")
        prm_T = sem("prm_T")
        prm_done = sem("prm_done")
        c_act = sem("c_act")
        xt_psum = sem("xt_psum")
        xt_done = sem("xt_done")
        ssq_x = sem("ssq_x")
        adas_in = [[sem(f"adas_in{b}_{q}") for q in range(2)] for b in range(ADA0)]
        adas_step = sem("adas_step")
        adas_sum = sem("adas_sum")
        mod_first = sem("mod_first")
        adaw_in = [sem(f"adaw_in{q}") for q in range(2)]
        adaw_used = [sem(f"adaw_used{q}") for q in range(2)]
        ada_step = sem("ada_step")
        ada_hi = sem("ada_hi")
        ada_lo = sem("ada_lo")
        onesr_made = sem("onesr_made")
        ada_sum = sem("ada_sum")
        modrow_out = sem("modrow_out")
        modrows_in = sem("modrows_in")
        mod_done = sem("mod_done")
        gs_done = sem("gs_done")
        cols_done = sem("cols_done")
        ms_done = sem("ms_done")
        pow_done = sem("pow_done")
        newton = sem("newton")
        diag_done = sem("diag_done")
        bc_done = sem("bc_done")
        tmp_done = sem("tmp_done")
        hH_done = sem("hH_done")
        hL_done = sem("hL_done")
        ssq_ps = sem("ssq_ps")
        silu_done = [[sem(f"silu{n}_{j}") for j in range(2)] for n in range(2)]
        prod_done = [[sem(f"prod{n}_{j}") for j in range(2)] for n in range(2)]
        actH_done = [sem(f"actH_done{n}") for n in range(2)]
        actL_done = [sem(f"actL_done{n}") for n in range(2)]
        x_done = [[sem(f"x_done{n}_{j}") for j in range(2)] for n in range(3)]
        sq_done = [sem(f"sq_done{n}") for n in range(3)]
        ssqa_done = [sem(f"ssqa_done{n}") for n in range(3)]
        d_free = [sem(f"d_free{b}") for b in range(2)]
        fa_sem = sem("fa_sem")
        fa_act = sem("fa_act")
        negF_done = sem("negF_done")
        negF_out = sem("negF_out")
        rel_in = sem("rel_in")
        relx_done = sem("relx_done")
        relx_out = sem("relx_out")
        relb_out = sem("relb_out")
        bias_in = sem("bias_in")
        qhi = sem("qhi")
        v_copied = sem("v_copied")
        v_turned = sem("v_turned")
        vhi = sem("vhi")
        s_done = sem("s_done")
        biased = sem("biased")
        exp_done = sem("exp_done")
        rinv_done = sem("rinv_done")
        p_ready = sem("p_ready")
        p_turned = sem("p_turned")
        pthi = sem("pthi")
        pt_ready = sem("pt_ready")
        pv_done = sem("pv_done")
        olo_part = [sem(f"olo_part{h}") for h in range(2)]
        o_summed = [sem(f"o_summed{h}") for h in range(2)]
        ohi = [sem(f"ohi{h}") for h in range(2)]
        o_ready = [sem(f"o_ready{h}") for h in range(2)]
        gates_done = sem("gates_done")
        y_done = sem("y_done")
        yadd_done = sem("yadd_done")
        yhi = sem("yhi")
        yH_ready = sem("yH_ready")
        xg_done = sem("xg_done")
        yt_done = [sem(f"yt_done{e}") for e in range(2)]
        y_ready = [sem(f"y_ready{e}") for e in range(2)]
        out_sent = sem("out_sent")

        def head_rows(h):
            return slice(DH * h, DH * h + DH)

        def turned_v(h):
            return bank[:, 1, :].rearrange("p (a b) -> p a b", a=TT)[:, :, head_rows(h)]

        def f32(ap):
            return ap.bitcast(F32)

        def landed(base, stride, i, k):
            return 16 * ((base + k) // 2 + 1) + i * (8 * stride)

        def tiles_of(w, cols, n=UT, k0=0):
            return w.rearrange("a (k p) n -> p (a k) n", p=P)[:, k0:k0 + n, cols]

        def sp_load(sp, base, stride, i, k, src):
            s = (base + k) % 2
            n, w = src.shape[1], src.shape[2]
            sp.wait_ge(lo_done, base + k - 1 + FREE + i * stride)
            sp.dma_start(raw[s][:, :n * w].rearrange("p (k n) -> p k n", k=n), src).then_inc(raw_in[s], 16)

        def sp_ada(sp, done, i, q, col, width):
            sp.wait_ge(adaw_used[q], done + i + START)
            src = ada_w.rearrange("a (p k) n -> p (a k) n", k=DT)[:, 4 * q:4 * q + 4, ds(col, width)]
            sp.dma_start(adaw[:, q, :, :width], src).then_inc(adaw_in[q], 16)

        def sp_ffn(sp, w_gate, w_up, w_down, u_gu, u_dn, ada):
            def gate_up(i, k0):
                for k in range(k0, 4):
                    w = (w_gate, w_up)[k % 2]
                    sp_load(sp, u_gu, 4, i, k, tiles_of(w, ds(i * 2 * P + (k // 2) * P, P)))
                    if ada and k >= 2:
                        sp_ada(sp, 0, i, k - 2, i * AC + ADA0 * AC, AC)

            if ada:
                gate_up(0, 2)
            with sp.Fori(int(ada), FT // 2) as i:
                gate_up(i, 0)
            with sp.Fori(0, DT // 2) as i:
                for k in range(6):
                    k0, n = PARTS[k % 3]
                    sp_load(sp, u_dn, 6, i, k, tiles_of(w_down, ds(i * 2 * P + (k // 3) * P, P), n, k0))
                    if ada and k < 2:
                        sp_ada(sp, ADA1, i, k, i * AC2 + (ADA0 + ADA1) * AC, AC2)

        def sp_pairs(sp, br):
            offs = QKV_OFF[br]
            with sp.Fori(0, PAIRS // 2) as i:
                for pp in range(2):
                    for k in range(5):
                        if k < 3:
                            cols = ds(i * 2 * P + offs[k] + pp * P, P)
                        else:
                            cols = ds(i * 4 * P + OFF_G + br * D + (2 * pp + k - 3) * P, P)
                        sp_load(sp, U_MIX[br], 10, i, 5 * pp + k, tiles_of(mix_w_in, cols))

        def sp_branch(sp, br):
            w = (branch_w_a, branch_w_b)[br]
            with sp.Fori(0, DT // 4) as i:
                for k in range(2):
                    sp_load(sp, U_BR[br], 2, i, k, tiles_of(w, ds(i * 4 * P + k * 2 * P, 2 * P), 4))

        def load_first_block(eng, b):
            for q in range(2):
                for m in range(2):
                    cols = slice(m * D + b * (AC // 2), m * D + (b + 1) * (AC // 2))
                    eng.dma_start(adas[:, b, 4 * q:4 * q + 4, m * (AC // 2):(m + 1) * (AC // 2)],
                                  ada_w.rearrange("a (p k) n -> p (a k) n", k=DT)[:, 4 * q:4 * q + 4, cols]
                                  ).then_inc(adas_in[b][q], 16)

        block = ctx.enter_context(nc.Block())

        @block.sync
        def _(sp):
            sp.dma_start(ccol[:, :], c.rearrange("a (p k) -> p (a k)", k=DT)).then_inc(c_in, 16)
            row = 0
            for src in (norm_ffn1, norm_mix, norm_ffn2, ada_b, branch_gate_b, final_norm.rearrange("(a n) -> a n", a=1)):
                n = src.shape[1] // P
                sp.dma_start(prm_in[row:row + n, :], src.rearrange("a (r n) -> (a r) n", n=P)).then_inc(prm_loaded, 16)
                row += n
            for t in range(TT):
                sp.dma_start(xin[:, t, :], x[0, t * P:(t + 1) * P, :]).then_inc(x_in[t], 16)
            sp.dma_start(fb[:, :], forget_b.rearrange("a h -> h a")).then_inc(fb_in, 16)
            load_first_block(sp, 1)
            for k in range(2):
                sp_load(sp, 0, 0, 0, k, tiles_of((ffn1_w_gate, ffn1_w_up)[k], slice(0, P)))
            load_first_block(sp, 2)
            load_first_block(sp, 3)
            sp_ffn(sp, ffn1_w_gate, ffn1_w_up, ffn1_w_down, U_GU1, U_DN1, True)
            sp_load(sp, U_FA, 0, 0, 0, tiles_of(mix_w_in, slice(OFF_F, OFF_F + P)))
            sp_pairs(sp, 0)
            sp_branch(sp, 0)
            sp_pairs(sp, 1)
            sp_branch(sp, 1)
            with sp.Fori(0, DT // 2) as i:
                for k in range(2):
                    sp_load(sp, U_OUT, 2, i, k, tiles_of(mix_w_out, ds(i * 2 * P + k * P, P)))
            sp_ffn(sp, ffn2_w_gate, ffn2_w_up, ffn2_w_down, U_GU2, U_DN2, False)
            for t in range(TT):
                for e in range(2):
                    sp.wait_ge(y_ready[e], t + 1)
                    cols = slice(e * SEQ, (e + 1) * SEQ)
                    sp.dma_start(out[0, t * P:(t + 1) * P, cols], y[:, t, cols]).then_inc(out_sent, 16)
            sp.wait_ge(out_sent, 16 * 2 * TT)

        @block.gpsimd
        def _(pool):
            pool.wait_ge(consts_v, 5)
            nc.gpsimd.affine_select(out=ident[:, :], in_=ident[:, :], compare_op=ALU.not_equal, fill=1.0, base=0,
                                    pattern=[[-1, P]], channel_multiplier=1).then_inc(ident_made, 1)
            nc.gpsimd.affine_select(out=mask[0][:, :], in_=mask[0][:, :], compare_op=ALU.is_ge, fill=NEG_INF, base=0,
                                    pattern=[[-1, P]], channel_multiplier=1).then_inc(masks_made, 1)
            def pair_biases(br):
                pool.wait_ge((negF_out, relb_out)[br], 16)
                with pool.Fori(0, PAIRS) as i:
                    pool.wait_ge(biased, i * 8 + 8 * PAIRS * br + START)
                    if br == 0:
                        src = negF_d[ds(i * 2, 2), :].partition_broadcast(P)
                    else:
                        src = relb_d.rearrange("h p s -> p h s")[:, ds(i * 2, 2), :]
                    pool.dma_start(bias[:, :, :], src).then_inc(bias_in, 16)

            for n in range(4):
                pool.wait_ge(ms_done, n + 1)
                nc.gpsimd.tensor_tensor(nrm[:, 1, :], nrm[:, 0, :], mhalf[:, :], ALU.pow).then_inc(pow_done, 1)
                if n == 0:
                    with pool.Fori(0, ADA1) as i:
                        pool.wait_ge(mod_done, i + 1 + START)
                        pool.dma_start(mod_d[:, ds(i * AC, AC)], modrow).then_inc(modrow_out, 16)
                    pool.wait_ge(modrow_out, 16 * ADA1)
                    pool.dma_start(modrows, mod_d.rearrange("a (r n) -> (a r) n", n=P)).then_inc(modrows_in, 16)
                if n == 1:
                    pool.wait_ge(unit_done, U_FA)
                    pool.dma_start(rel[:, :], rel_bias[0, :, :]).then_inc(rel_in, 16)
                    pool.wait_ge(negF_done, 1)
                    pool.dma_start(negF_d, fgate[:, 5, :]).then_inc(negF_out, 16)
                    pair_biases(0)
                    pool.wait_ge(relx_done, 2)
                    pool.dma_start(relx_d, relx[:, :]).then_inc(relx_out, 16)
                    pool.wait_ge(relx_out, 16)
                    pool.dma_start(relb_d, bass.AP(relx_d.tensor, P, [[SEQ + P, HB], [-1, P], [1, SEQ]])).then_inc(relb_out, 16)
                    pair_biases(1)

        @block.scalar
        def _(act):
            def wait_apart(s, v):
                act.wait_ge(s, v)

            def prep(base, stride, i, k, n=UT):
                u = base + k
                if u >= U_END:
                    return
                s = u % 2
                act.wait_ge(raw_in[s], landed(base, stride, i, k))
                if u >= 2:
                    act.wait_ge(unit_done, u - 1 + i * stride)
                nc.scalar.activation(wH[s][:, :n * P], raw[s][:, :n * P], ACT.Copy).then_inc(hi_done, 1)

            def normed(n):
                for d in range(DT):
                    act.wait_ge(tmp_done, n * DT + d + 1)
                    nc.scalar.activation(hH[:, d, :], tmp[:, d % 2, :], ACT.Identity,
                                         bias=mod[:, M_SH[n] + d:M_SH[n] + d + 1]).then_inc(hH_done, 1)

            def gate_up(n, u0, ada):
                with act.Fori(0, FT // 2) as i:
                    for k in range(4):
                        if ada and k == 3:
                            act.wait_ge(ada_step, i * DT + DT)
                            nc.scalar.activation(adacH[:, :], adac[:, :], ACT.Copy).then_inc(ada_hi, 1)
                        prep(u0, 4, i, k + 2)
                        j = k // 2
                        if k % 2 == 0:
                            act.wait_ge(prod_done[n][j], i + START)
                            act.wait_ge(unit_done, i * 4 + u0 + k + 1)
                            nc.scalar.activation(sg[:, j, :], bank[:, k, :], ACT.Silu).then_inc(silu_done[n][j], 1)
                        else:
                            wait_apart(prod_done[n][j], i + 1 + START)
                            nc.scalar.activation(actH[:, ds(i * 2 + j, 1), :], pr[:, j:j + 1, :], ACT.Copy).then_inc(actH_done[n], 1)

            def squares(m, j, i):
                act.wait_ge(ssqa_done[m], i * 2 + j + START)
                wait_apart(x_done[m][j], i + 1 + START)
                nc.scalar.activation(tmp[:, j:j + 1, :], xT[:, ds(i * 2 + j, 1), :], ACT.Square).then_inc(sq_done[m], 1)

            def down(n, m, u0):
                def body(i):
                    for k in range(6):
                        if not (isinstance(i, int) and n == 1 and k >= 4):
                            prep(u0, 6, i, k + 2, PARTS[(k + 2) % 3][1])
                        if k % 3 == 2:
                            squares(m, k // 3, i)
                            if n == 1:
                                t = ds(i * 2 + k // 3, 1)
                                nc.scalar.activation(xg[:, t, :], xT[:, t, :], ACT.Copy,
                                                     scale=prm[:, ds(i * 2 + (C_NF + k // 3), 1)]).then_inc(xg_done, 1)
                with act.Fori(0, DT // 2 - n) as i:
                    body(i)
                if n == 1:
                    body(DT // 2 - 1)

            def forget_logs():
                act.wait_ge(fa_act, 2)
                nc.scalar.activation(fgate[:, 2, :], fgate[:, 1, :], ACT.Ln, bias=1.0).then_inc(fa_act, 1)
                act.wait_ge(fa_act, 3)
                nc.scalar.activation(fgate[:, 4, :], fgate[:, 2, :], ACT.Exp, scale=-1.0).then_inc(fa_act, 1)

            def pairs(br):
                u0 = U_MIX[br]

                def body(i, first=False):
                    for pp in range(2):
                        g = i * 2 + (4 * br + pp)
                        k0 = 5 * pp
                        for k, dst, sc in ((0, qHH, SCALE), (1, kHL, 1.0)):
                            prep(u0, 10, i, k0 + k + 2)
                            act.wait_ge(s_done, g * 8 + START)
                            act.wait_ge(unit_done, i * 10 + u0 + k0 + k + 1)
                            for other in range(2 - k):
                                for h in range(2):
                                    nc.scalar.activation(dst[head_rows(h ^ other), h, :], bank[head_rows(h), k, :], ACT.Copy,
                                                         scale=sc).then_inc(qhi, 1)
                            if first and pp == k == 0:
                                forget_logs()
                        act.wait_ge(unit_done, i * 10 + u0 + k0 + 3)
                        nc.scalar.activation(vT[:, :], bank[:, 0, :], ACT.Copy).then_inc(v_copied, 1)
                        prep(u0, 10, i, k0 + 4)
                        for h in range(2):
                            for n, t in enumerate(T_ORDER):
                                w = P * (t + 1)
                                act.wait_ge(biased, g * 8 + (4 * h + n + 1) + START)
                                nc.scalar.activation(prob[:, h, T_OFF[t]:T_OFF[t] + w], prob[:, h, T_OFF[t]:T_OFF[t] + w],
                                                     ACT.Exp, scale=-1.0, bias=negmax[:, h, t:t + 1],
                                                     accum_out=rowsum[:, h, t:t + 1]).then_inc(exp_done, 1)
                            if h == 0:
                                act.wait_ge(v_turned, g + 1)
                                for e in range(2):
                                    nc.scalar.activation(vHL[:, e, :, head_rows(e)], turned_v(e), ACT.Copy).then_inc(vhi, 1)

                        def gate(n):
                            wait_apart(unit_done, i * 10 + u0 + k0 + 4 + n)
                            col = i * 4 + C_GB + br * DT + 2 * pp + n
                            nc.scalar.activation(gbuf[:, ds(i * 4 + 2 * pp + n, 1), :], bank[:, n:n + 1, :], ACT.Identity,
                                                 bias=prm[:, ds(col, 1)]).then_inc(d_free[n], 1)

                        def turned_hi(h):
                            act.wait_ge(pv_done, g * 2 + h + START)
                            for n, cols in enumerate(PIECE_COLS):
                                act.wait_ge(p_turned, g * 4 + (2 * h + n + 1))
                                sbk = S_BANK[h]
                                nc.scalar.activation(ptH[:, cols], bank[:, sbk:sbk + 3, :].rearrange("p a b -> p (a b)")[:, cols],
                                                     ACT.Copy).then_inc(pthi, 1)

                        def out_part(h):
                            act.wait_ge(o_ready[h], g + START)
                            act.wait_ge(pv_done, g * 2 + h + 1 + START)
                            nc.scalar.activation(osum[head_rows(h), :], bank[head_rows(1 - h), S_BANK[h], :],
                                                 ACT.Copy).then_inc(olo_part[h], 1)

                        def out_hi(h):
                            wait_apart(o_summed[h], g + 1)
                            nc.scalar.activation(oH[head_rows(h), ds(i * 2 + pp, 1), :],
                                                 osum[head_rows(h), :].rearrange("p (a n) -> p a n", a=1), ACT.Copy).then_inc(ohi[h], 1)

                        turned_hi(0)
                        prep(u0, 10, i, k0 + 5)
                        if br == 1:
                            act.wait_ge(y_done, DT + Y_START)
                        gate(0)
                        out_part(0)
                        turned_hi(1)
                        out_hi(0)
                        prep(u0, 10, i, k0 + 6)
                        gate(1)
                        out_part(1)
                        out_hi(1)

                if br == 0:
                    body(0, True)
                with act.Fori(1 - br, PAIRS // 2) as i:
                    body(i)

            def branch(br):
                act.wait_ge(d_free[0], 1 + 3 * PAIRS * (br + 1))
                act.wait_ge(d_free[1], 5 * PAIRS * (br + 1) + START)
                for d in range(DT):
                    nc.scalar.activation(gbuf[:, d, :], gbuf[:, d, :], ACT.Sigmoid).then_inc(gates_done, 1)
                with act.Fori(0, DT // 4) as i:
                    for k in range(2):
                        prep(U_BR[br], 2, i, k + 2)
                        if br == 1:
                            for e in range(2):
                                t = ds(i * 4 + 2 * k + e, 1)
                                wait_apart(yadd_done, i * 4 + (2 * k + e + 1))
                                nc.scalar.activation(hH[:, t, :], ymix[:, t, :], ACT.Copy).then_inc(yhi, 1)

            for first in silu_done[0] + silu_done[1]:
                act.sem_inc(first, START)
            load_first_block(act, 0)
            act.wait_ge(c_in, 16)
            nc.scalar.activation(csilu[:, :], ccol[:, :], ACT.Silu).then_inc(c_act, 1)
            act.wait_ge(prm_T, 1)
            nc.scalar.activation(prm[:, :N_PRM], bank[:, 0, :N_PRM], ACT.Copy).then_inc(prm_done, 1)
            for t in range(TT):
                act.wait_ge(x_in[t], 16)
                if t >= 1:
                    act.wait_ge(ssq_x, t)
                nc.scalar.activation(sqx[:, :], xin[:, t, :], ACT.Square, accum_out=ssq0[:, t:t + 1]).then_inc(ssq_x, 1)
            for d in range(DT):
                act.wait_ge(xt_psum, d + 1)
                nc.scalar.activation(xT[:, d, :], bank[:, 1 + d % 2, :], ACT.Copy).then_inc(xt_done, 1)
            for k in range(2):
                prep(0, 0, 0, k)
            normed(0)
            gate_up(0, U_GU1, True)
            down(0, 0, U_DN1)
            normed(1)
            prep(U_FA, 0, 0, 2)
            act.wait_ge(unit_done, U_FA + 1)
            nc.scalar.activation(fgate[:, 0, :], bank[0:HA, B_FA, :], ACT.Abs, bias=fb[:, :]).then_inc(fa_act, 1)
            nc.scalar.activation(fgate[:, 3, :], bank[0:HA, B_FA, :], ACT.Relu, bias=nfb[:, :], scale=-1.0).then_inc(d_free[0], 1)
            act.wait_ge(fa_act, 1)
            nc.scalar.activation(fgate[:, 1, :], fgate[:, 0, :], ACT.Exp, scale=-1.0).then_inc(fa_act, 1)
            pairs(0)
            branch(0)
            pairs(1)
            branch(1)
            with act.Fori(0, DT // 2) as i:
                for k in range(2):
                    prep(U_OUT, 2, i, k + 2)
                    squares(1, k, i)
            normed(2)
            gate_up(1, U_GU2, False)
            down(1, 2, U_DN2)
            act.wait_ge(newton, 3 * 4)
            for t in range(TT):
                act.wait_ge(yt_done[0], t + 1)
                nc.scalar.activation(y[:, t, :SEQ], bank[:, Y_BANK[0][t], :], ACT.Copy,
                                     scale=nrm[:, 4, t:t + 1]).then_inc(y_ready[0], 1)

        @block.vector
        def _(dve):
            V = nc.vector

            def wait_apart(s, v, at):
                dve.wait_ge(s, v)
                V.memset(at, 0.0)

            def prep(base, stride, i, k, n=UT):
                u = base + k
                if u >= U_END:
                    return
                s = u % 2
                dve.wait_ge(hi_done, u + 1 + i * stride)
                V.tensor_tensor(wL[s][:, :n * P], raw[s][:, :n * P], f32(wH[s][:, :n * P]), ALU.subtract).then_inc(lo_done, 1)

            def ada_rows(done, i, rows, width, acc):
                for k in rows:
                    q, r = k // 4, k % 4
                    if r == 0:
                        dve.wait_ge(adaw_in[q], i * 16 + 16 * (done + 1))
                    if k == 0:
                        ins = V.tensor_scalar(acc, adaw[:, q, r:r + 1, :width], csilu[:, 0:1], None, ALU.mult)
                    else:
                        dve.wait_ge(ada_step, i * 8 + (8 * done + k))
                        ins = V.scalar_tensor_tensor(out=acc, in0=adaw[:, q, r:r + 1, :width], scalar=csilu[:, k:k + 1],
                                                     in1=acc, op0=ALU.mult, op1=ALU.add)
                    ins.then_inc(ada_step, 1)
                    if r == 3:
                        dve.wait_ge(ada_step, i * 8 + (8 * done + 4 * q + 4))
                        dve.sem_inc(adaw_used[q], 1)

            def ada_row(i):
                dve.wait_ge(ada_sum, i + 1)
                if not isinstance(i, int):
                    dve.wait_ge(modrow_out, i * 16)
                V.tensor_copy(modrow, bank[0:1, B_ADA, :]).then_inc(mod_done, 1)

            def rstd(n):
                if n == 0:
                    dve.wait_ge(ssq_x, TT)
                    src = ssq0[:, :]
                else:
                    dve.wait_ge(ssq_ps, n)
                    src = bank[:, B_SSQ, 0:TT]
                V.tensor_scalar(nrm[:, 0, :], src, 1.0 / D, EPS, ALU.mult, ALU.add).then_inc(ms_done, 1)
                dve.wait_ge(pow_done, n + 1)
                V.scalar_tensor_tensor(out=nrm[:, 2, :], in0=nrm[:, 1, :], scalar=-0.5, in1=nrm[:, 1, :],
                                       op0=ALU.mult, op1=ALU.mult).then_inc(newton, 1)
                dve.wait_ge(newton, 3 * n + 1)
                V.tensor_tensor(nrm[:, 3, :], nrm[:, 2, :], nrm[:, 0, :], ALU.mult).then_inc(newton, 1)
                dve.wait_ge(newton, 3 * n + 2)
                V.scalar_tensor_tensor(out=nrm[:, 4, :], in0=nrm[:, 3, :], scalar=1.5, in1=nrm[:, 1, :],
                                       op0=ALU.add, op1=ALU.mult).then_inc(newton, 1)
                dve.wait_ge(newton, 3 * n + 3)

            def normed(n):
                rstd(n)
                V.tensor_tensor(diag[:, :, :], ident[:, :].rearrange("p (a b) -> p a b", a=1).to_broadcast([P, TT, P]),
                                nrm[:, 4, :].rearrange("p (a b) -> p a b", b=1).to_broadcast([P, TT, P]),
                                ALU.mult).then_inc(diag_done, 1)
                if n == 0:
                    for k in range(2):
                        prep(0, 0, 0, k)
                dve.wait_ge(bc_done, n + 1)
                if n == 0:
                    dve.wait_ge(xt_done, DT)
                else:
                    dve.wait_ge(gs_done, n)
                for b in range(DT // 2):
                    if n == 0:
                        if b >= 1 and b + 1 < ADA0:
                            first_rows(b + 1)
                        first_columns(b)
                    for d in (2 * b, 2 * b + 1):
                        if b >= 1:
                            dve.wait_ge(hL_done, n * DT + d - 1)
                        V.scalar_tensor_tensor(out=tmp[:, d % 2, :], in0=xT[:, d, :], scalar=gs[:, n, d:d + 1],
                                               in1=bank[:, B_BC, :], op0=ALU.mult, op1=ALU.mult).then_inc(tmp_done, 1)
                    for d in (2 * b, 2 * b + 1):
                        dve.wait_ge(hH_done, n * DT + d + 1)
                        V.scalar_tensor_tensor(out=hL[:, d, :], in0=tmp[:, d % 2, :], scalar=mod[:, M_SH[n] + d:M_SH[n] + d + 1],
                                               in1=f32(hH[:, d, :]), op0=ALU.add, op1=ALU.subtract).then_inc(hL_done, 1)

            def first_rows(b):
                for k in range(ROWS_V[b]):
                    if k % 4 == 0:
                        dve.wait_ge(adas_in[b][k // 4], 32)
                    if k == 0:
                        ins = V.tensor_scalar(adasc[:, b, :], adas[:, b, 0, :], csilu[:, 0:1], None, ALU.mult)
                    else:
                        dve.wait_ge(adas_step, sum(ROWS_V[:b]) + k)
                        ins = V.scalar_tensor_tensor(out=adasc[:, b, :], in0=adas[:, b, k, :], scalar=csilu[:, k:k + 1],
                                                     in1=adasc[:, b, :], op0=ALU.mult, op1=ALU.add)
                    ins.then_inc(adas_step, 1)

            def first_columns(b):
                def pick(t, c0, stride):
                    return t[:, c0:c0 + 2 * stride].rearrange("p (a d) -> p a d", a=2)
                dve.wait_ge(adas_sum, b + 1)
                out = pick(mod, 0, DT)[:, :, 2 * b:2 * b + 2]
                sums = bank[:, B_ADA_START[b], 0:8].rearrange("p (s a d) -> p s a d", s=2, a=2)
                V.tensor_tensor(out, sums[:, 0], pick(prm, C_AB, DT)[:, :, 2 * b:2 * b + 2], ALU.add).then_inc(mod_first, 1)
                dve.wait_ge(mod_first, 3 * b + 1)
                V.tensor_tensor(out, sums[:, 1], out, ALU.add).then_inc(mod_first, 1)
                dve.wait_ge(mod_first, 3 * b + 2)
                V.scalar_tensor_tensor(out=gs[:, 0, 2 * b:2 * b + 2], in0=mod[:, DT + 2 * b:DT + 2 * b + 2], scalar=1.0,
                                       in1=prm[:, C_N1 + 2 * b:C_N1 + 2 * b + 2], op0=ALU.add, op1=ALU.mult).then_inc(mod_first, 1)
                dve.wait_ge(mod_first, 3 * b + 3)
                if b == ADA0 - 2:
                    for q in range(2):
                        dve.sem_inc(adaw_used[q], START)

            def scale_columns(n, g_col):
                V.scalar_tensor_tensor(out=gs[:, n, :], in0=mod[:, M_SC[n]:M_SC[n] + DT], scalar=1.0,
                                       in1=prm[:, g_col:g_col + DT], op0=ALU.add, op1=ALU.mult).then_inc(gs_done, 1)

            def gate_up(n, u0, ada):
                def body(i):
                    for k in range(4):
                        j = k // 2
                        if ada and k == 3:
                            dve.wait_ge(ada_hi, i + 1)
                            V.tensor_tensor(adacL[:, :], adac[:, :], f32(adacH[:, :]), ALU.subtract).then_inc(ada_lo, 1)
                        if k % 2:
                            dve.wait_ge(silu_done[n][j], i + 1 + START)
                            dve.wait_ge(unit_done, i * 4 + u0 + k + 1)
                            dve.wait_ge(actL_done[n], i * 2 + START)
                            V.tensor_tensor(pr[:, j, :], sg[:, j, :], bank[:, k, :], ALU.mult).then_inc(prod_done[n][j], 1)
                        prep(u0, 4, i, k + 2)
                        if k % 2:
                            dve.wait_ge(actH_done[n], i * 2 + j + 1)
                            V.tensor_tensor(actL[:, ds(i * 2 + j, 1), :], pr[:, j:j + 1, :], f32(actH[:, ds(i * 2 + j, 1), :]),
                                            ALU.subtract).then_inc(actL_done[n], 1)
                        if ada and k < 3:
                            ada_rows(0, i, (range(4), range(4, 7), range(7, 8))[k], AC,
                                     adac[:, :].rearrange("p (a n) -> p a n", a=1))
                        if ada and k == 3:
                            ada_row(i)

                if ada:
                    body(0)
                with dve.Fori(int(ada), FT // 2) as i:
                    body(i)

            def residual(m, j, i, b, u):
                dve.wait_ge(unit_done, u)
                V.scalar_tensor_tensor(out=xT[:, ds(i * 2 + j, 1), :], in0=bank[:, b:b + 1, :],
                                       scalar=gres[:, m, ds(i * 2 + j, 1)], in1=xT[:, ds(i * 2 + j, 1), :],
                                       op0=ALU.mult, op1=ALU.add).then_inc(x_done[m][j], 1)

            def add_squares(m, j, i):
                dve.wait_ge(sq_done[m], i * 2 + j + 1)
                dve.wait_ge(ssqa_done[m], i * 2 + j + START)
                V.tensor_tensor(ssqa[:, :], ssqa[:, :], tmp[:, j, :], ALU.add).then_inc(ssqa_done[m], 1)

            def down(n, m, u0, ada):
                def columns():
                    c0, c1 = ADA0 * AC // P, (ADA0 + ADA1) * AC // P
                    dve.wait_ge(ada_sum, ADA1 + 1)
                    V.tensor_tensor(mod[:, c0:c1], bank[:, B_ADA, 0:c1 - c0], prm[:, C_AB + c0:C_AB + c1], ALU.add).then_inc(mod_done, 1)
                    dve.wait_ge(mod_done, ADA1 + 1 + START)
                    V.tensor_scalar(gres[:, 0, :], mod[:, M_G[0]:M_G[0] + DT], 0.5, None, ALU.mult).then_inc(cols_done, 1)
                    scale_columns(1, C_NM)
                    V.tensor_copy(gres[:, 1, :], mod[:, M_G[1]:M_G[1] + DT]).then_inc(cols_done, 1)
                    dve.wait_ge(cols_done, 3)

                def body(i):
                    for k in range(6):
                        if ada and isinstance(i, int) and k == 2:
                            columns()
                        if k % 3 == 2:
                            residual(m, k // 3, i, 5 + k // 3, i * 6 + u0 + k + 1)
                        if not (isinstance(i, int) and n == 1 and k >= 4):
                            prep(u0, 6, i, k + 2, PARTS[(k + 2) % 3][1])
                        if k % 3 == 2:
                            add_squares(m, k // 3, i)
                        if ada and k in (1, 3):
                            ada_rows(ADA1, i, range(4 * (k // 2), 4 * (k // 2) + 4), AC2, adac2[:, ds(i, 1), :])
                if ada:
                    body(0)
                with dve.Fori(int(ada), DT // 2 - n) as i:
                    body(i)
                if n == 1:
                    body(DT // 2 - 1)

            def forget_sums():
                z = fgate
                dve.wait_ge(fa_act, 3)
                dve.wait_ge(d_free[0], 3)
                dve.wait_ge(fa_sem, 3)
                V.tensor_tensor(z[:, 0, :], z[:, 2, :], z[:, 3, :], ALU.add).then_inc(fa_sem, 1)
                dve.wait_ge(fa_act, 4)
                V.tensor_tensor(z[:, 5, :], z[:, 5, :], z[:, 4, :], ALU.mult).then_inc(fa_sem, 1)
                dve.wait_ge(fa_sem, 5)
                V.tensor_tensor(z[:, 0, :], z[:, 0, :], z[:, 5, :], ALU.add).then_inc(fa_sem, 1)
                dve.wait_ge(fa_sem, 6)
                V.tensor_tensor_scan(z[:, 5, :], ones[0:HA, 0:1].to_broadcast([HA, SEQ]), z[:, 0, :], 0.0,
                                     ALU.mult, ALU.add).then_inc(negF_done, 1)

            def pairs(br):
                u0 = U_MIX[br]

                def body(i, first=False):
                    for pp in range(2):
                        g = i * 2 + (4 * br + pp)
                        k0 = 5 * pp
                        prep(u0, 10, i, k0 + 2)
                        for h in range(2):
                            dve.wait_ge(qhi, g * 6 + 4)
                            V.scalar_tensor_tensor(out=qL[head_rows(h), :], in0=bank[head_rows(h), 0, :], scalar=SCALE,
                                                   in1=f32(qHH[head_rows(h), h, :]), op0=ALU.mult, op1=ALU.subtract).then_inc(d_free[0], 1)
                        if first and pp == 0:
                            forget_sums()
                        for h in range(2):
                            dve.wait_ge(qhi, g * 6 + 5 + h)
                            V.tensor_tensor(kHL[head_rows(1 - h), h, :], bank[head_rows(h), 1, :], f32(kHL[head_rows(h), h, :]),
                                            ALU.subtract).then_inc(d_free[1], 1)
                        prep(u0, 10, i, k0 + 3)
                        prep(u0, 10, i, k0 + 4)

                        def biased_scores(h):
                            for n, t in enumerate(T_ORDER):
                                w = P * (t + 1)
                                b0 = (0, SEQ - w)[br]
                                if n == 0:
                                    dve.wait_ge(bias_in, g * 16 + 16)
                                wait_apart(s_done, g * 8 + (h + (1, 5, 5, 7)[n]) + START, spare[:, 4 * h + n:4 * h + n + 1])
                                V.tensor_tensor_reduce(
                                    out=prob[:, h, T_OFF[t]:T_OFF[t] + w],
                                    in0=bank[:, S_BANK[h]:S_BANK[h] + 3, :].rearrange("p a b -> p (a b)")[:, T_OFF[t]:T_OFF[t] + w],
                                    in1=bias[:, h, b0:b0 + w], scale=-1.0, scalar=BIG, op0=ALU.add, op1=ALU.min,
                                    accum_out=negmax[:, h, t:t + 1]).then_inc(biased, 1)

                        def normalised(h):
                            dve.wait_ge(exp_done, g * 8 + (4 * h + 4))
                            V.reciprocal(rinv[:, h, :], rowsum[:, h, :]).then_inc(rinv_done, 1)
                            dve.wait_ge(rinv_done, g * 2 + h + 1)
                            for n, t in enumerate(T_ORDER):
                                a = prob[:, h, T_OFF[t]:T_OFF[t] + P * (t + 1)]
                                V.tensor_scalar(a, a, rinv[:, h, t:t + 1], None, ALU.mult).then_inc(p_ready, 1)

                        def turned_lo(h):
                            for n, cols in enumerate(PIECE_COLS):
                                dve.wait_ge(pthi, g * 4 + (2 * h + n + 1))
                                V.tensor_tensor(ptL[:, cols], bank[:, S_BANK[h]:S_BANK[h] + 3, :].rearrange("p a b -> p (a b)")[:, cols],
                                                f32(ptH[:, cols]), ALU.subtract).then_inc(pt_ready, 1)

                        def out_sum(h):
                            rows = head_rows(h)
                            dve.wait_ge(olo_part[h], g + 1)
                            V.tensor_tensor(osum[rows, :], bank[rows, S_BANK[h], :], osum[rows, :], ALU.add).then_inc(o_summed[h], 1)

                        def out_lo(h):
                            rows = head_rows(h)
                            dve.wait_ge(ohi[h], g + 1)
                            V.tensor_tensor(oL[rows, ds(i * 2 + pp, 1), :], osum[rows, :].rearrange("p (a n) -> p a n", a=1),
                                            f32(oH[rows, ds(i * 2 + pp, 1), :]), ALU.subtract).then_inc(o_ready[h], 1)

                        biased_scores(0)
                        biased_scores(1)
                        normalised(0)
                        dve.wait_ge(vhi, g * 2 + 2)
                        for e in range(2):
                            V.tensor_tensor(vHL[:, e, :, head_rows(1 - e)], turned_v(e), f32(vHL[:, e, :, head_rows(e)]),
                                            ALU.subtract).then_inc(d_free[1], 1)
                        normalised(1)
                        turned_lo(0)
                        prep(u0, 10, i, k0 + 5)
                        out_sum(0)
                        turned_lo(1)
                        out_lo(0)
                        prep(u0, 10, i, k0 + 6)
                        out_sum(1)
                        out_lo(1)

                if br == 0:
                    body(0, True)
                with dve.Fori(1 - br, PAIRS // 2) as i:
                    body(i)

            def branch(br):
                u0 = U_BR[br]
                with dve.Fori(0, DT // 4) as i:
                    for k in range(2):
                        dve.wait_ge(unit_done, i * 2 + u0 + k + 1)
                        for e in range(2):
                            t = ds(i * 4 + 2 * k + e, 1)
                            dve.wait_ge(gates_done, i * 4 + (DT * br + 2 * k + e + 1))
                            if br == 0:
                                V.tensor_tensor(ymix[:, t, :], bank[:, 2 + 2 * k + e:3 + 2 * k + e, :], gbuf[:, t, :],
                                                ALU.mult).then_inc(y_done, 1)
                            else:
                                V.tensor_tensor(gbuf[:, t, :], bank[:, 2 + 2 * k + e:3 + 2 * k + e, :], gbuf[:, t, :],
                                                ALU.mult).then_inc(y_done, 1)
                        if br == 1:
                            for e in range(2):
                                t = ds(i * 4 + 2 * k + e, 1)
                                dve.wait_ge(y_done, i * 4 + DT + 2 * k + e + 1 + Y_START)
                                V.tensor_tensor(ymix[:, t, :], ymix[:, t, :], gbuf[:, t, :], ALU.add).then_inc(yadd_done, 1)
                        prep(u0, 2, i, k + 2)
                        if br == 1:
                            for e in range(2):
                                t = ds(i * 4 + 2 * k + e, 1)
                                dve.wait_ge(yhi, i * 4 + (2 * k + e + 1))
                                V.tensor_tensor(hL[:, t, :], ymix[:, t, :], f32(hH[:, t, :]), ALU.subtract).then_inc(yH_ready, 1)

            dve.sem_inc(lo_done, FREE)
            for first in (prod_done[0] + prod_done[1] + [mod_done] + x_done[0] + x_done[1] + x_done[2]
                          + actL_done + ssqa_done + [biased, d_free[1]] + o_ready):
                dve.sem_inc(first, START)
            dve.sem_inc(y_done, Y_START)
            V.memset(ident[:, :], 0.0).then_inc(consts_v, 1)
            V.memset(mask[0][:, :], 0.0).then_inc(consts_v, 1)
            V.memset(mask[1][:, :], 0.0).then_inc(consts_v, 1)
            V.memset(ones[:, :], 1.0).then_inc(consts_v, 1)
            V.memset(mhalf[:, :], -0.5).then_inc(consts_v, 1)
            dve.wait_ge(consts_v, 3)
            V.memset(mask[1][0:64, 64:P], NEG_INF).then_inc(masks_made, 1)
            dve.wait_ge(consts_v, 4)
            V.tensor_copy(onesr[:, :], ones[:, 0:2]).then_inc(onesr_made, 1)
            dve.wait_ge(ident_made, 1)
            V.tensor_copy(identb[:, :], ident[:, :]).then_inc(identb_made, 1)
            dve.wait_ge(c_act, 1)
            first_rows(0)
            first_rows(1)
            dve.wait_ge(fb_in, 16)
            V.tensor_scalar(nfb[:, :], fb[:, :], -1.0, None, ALU.mult).then_inc(fa_sem, 1)
            dve.wait_ge(prm_done, 1)
            normed(0)
            gate_up(0, U_GU1, True)
            V.memset(ssqa[:, :], 0.0).then_inc(cols_done, 1)
            down(0, 0, U_DN1, True)
            normed(1)
            dve.wait_ge(ada_sum, ADA1 + 2)
            V.tensor_tensor(mod[:, N_MOD * DT - N_LAST:], bank[:, B_LAST, 0:N_LAST],
                            prm[:, C_AB + N_MOD * DT - N_LAST:C_AB + N_MOD * DT], ALU.add).then_inc(mod_done, 1)
            dve.wait_ge(mod_done, ADA1 + 2 + START)
            scale_columns(2, C_N2)
            V.tensor_scalar(gres[:, 2, :], mod[:, M_G[2]:M_G[2] + DT], 0.5, None, ALU.mult).then_inc(cols_done, 1)
            prep(U_FA, 0, 0, 2)
            dve.wait_ge(fa_act, 2)
            V.tensor_scalar(fgate[:, 0, :], fgate[:, 1, :], 1.0, -1.0, ALU.add, ALU.add).then_inc(fa_sem, 1)
            dve.wait_ge(fa_sem, 2)
            V.tensor_tensor(fgate[:, 5, :], fgate[:, 1, :], fgate[:, 0, :], ALU.subtract).then_inc(fa_sem, 1)
            pairs(0)
            dve.wait_ge(rel_in, 16)
            half = SEQ + P - (N_REL - 1)
            V.tensor_copy(relx[:, :half], rel[:, N_REL - 1:N_REL].to_broadcast([HB, half])).then_inc(relx_done, 1)
            V.tensor_copy(relx[:, half:], rel[:, N_REL - 1:0:-1]).then_inc(relx_done, 1)
            V.memset(ssqa[:, :], 0.0).then_inc(cols_done, 1)
            branch(0)
            pairs(1)
            branch(1)
            with dve.Fori(0, DT // 2) as i:
                for k in range(2):
                    residual(1, k, i, k, i * 2 + U_OUT + k + 1)
                    prep(U_OUT, 2, i, k + 2)
                    add_squares(1, k, i)
            normed(2)
            gate_up(1, U_GU2, False)
            V.memset(ssqa[:, :], 0.0).then_inc(cols_done, 1)
            dve.wait_ge(cols_done, 6)
            down(1, 2, U_DN2, False)
            rstd(3)
            for t in range(TT):
                dve.wait_ge(yt_done[1], t + 1)
                V.tensor_scalar(y[:, t, SEQ:], bank[:, Y_BANK[1][t], :], nrm[:, 4, t:t + 1], None,
                                ALU.mult).then_inc(y_ready[1], 1)

        @block.tensor
        def _(pe):
            T = nc.tensor

            def three(o, a, b, start, stop):
                T.matmul(o, a[0], b[0], start=start, stop=False)
                T.matmul(o, a[0], b[1], start=False, stop=False)
                return T.matmul(o, a[1], b[0], start=False, stop=stop)

            def tile(s, k):
                return wH[s][:, k * P:(k + 1) * P], wL[s][:, k * P:(k + 1) * P]

            def dense(u, s, o, rhs, ks, first, last, at=0):
                if at == 0:
                    pe.wait_ge(lo_done, u + 1 + FREE)
                for n, k in enumerate(ks):
                    ins = three(o, tile(s, at + n), (rhs[0][:, k, :], rhs[1][:, k, :]), first and n == 0,
                                last and n == len(ks) - 1)
                return ins

            h = (hH, hL)
            a = (actH, actL)
            o_ = (oH, oL)

            def h_unit(u, s, o, ks=range(DT)):
                return dense(u, s, o, h, ks, ks[0] == 0, ks[-1] == DT - 1, ks[0])

            def first_parts(b):
                for q in range(2):
                    pe.wait_ge(adas_in[b][q], 32)
                for n in range(AC // P):
                    for r in range(ROWS_V[b], DT):
                        T.matmul(bank[:, B_ADA_START[b], 4 + n:5 + n], adas[:, b, r, n * P:(n + 1) * P],
                                 csilu[:, r:r + 1], start=r == ROWS_V[b], stop=r == DT - 1)

            def first_sums(b):
                pe.wait_ge(adas_step, sum(ROWS_V[:b + 1]))
                for n in range(AC // P):
                    ins = T.matmul(bank[:, B_ADA_START[b], n:n + 1], adasc[:, b, n * P:(n + 1) * P], ones[:, 0:1],
                                   start=True, stop=True)
                ins.then_inc(adas_sum, 1)

            def two_units(u, banks, ready):
                LAG = 3
                for k in range(DT + LAG):
                    if ready == 0 and k in (2, 4):
                        first_parts(k // 2 + 1)
                        first_sums(k // 2 + 1)
                    for n in range(2):
                        t = k - n * LAG
                        if 0 <= t < DT:
                            if t == 0:
                                pe.wait_ge(lo_done, u + n + 1 + FREE)
                            if n == 0:
                                pe.wait_ge(hL_done, ready + t + 1)
                            ins = three(bank[:, banks[n], :], tile((u + n) % 2, t), (hH[:, t, :], hL[:, t, :]), t == 0, t == DT - 1)
                            if t == DT - 1:
                                ins.then_inc(unit_done, 1)

            def ada_sums(i):
                pe.wait_ge(ada_lo, i + 1)
                pe.wait_ge(mod_done, i + START)
                T.matmul(bank[0:1, B_ADA, :], onesr[:, 0:1], adacH[:, :], start=True, stop=False)
                T.matmul(bank[0:1, B_ADA, :], onesr[:, 0:1], adacL[:, :], start=False, stop=True).then_inc(ada_sum, 1)

            def last_sums(cols):
                pe.wait_ge(ada_step, DT * (ADA1 + ADA2))
                for n in cols:
                    b, e = n // (AC2 // P), n % (AC2 // P)
                    ins = T.matmul(bank[:, B_LAST, n:n + 1], adac2[:, b, e * P:(e + 1) * P], ones[:, 0:1], start=True, stop=True)
                return ins

            def token_squares(m):
                pe.wait_ge(ssqa_done[m], DT + START)
                for t in range(TT):
                    ins = T.matmul(bank[:, B_SSQ, t:t + 1], ssqa[:, t * P:(t + 1) * P], ones[:, 0:1], start=True, stop=True)
                ins.then_inc(ssq_ps, 1)

            def spread(n):
                pe.wait_ge(diag_done, n + 1)
                for t in range(TT):
                    ins = T.matmul(bank[:, B_BC, t * P:(t + 1) * P], ones[:, :], diag[:, t, :], start=True, stop=True)
                ins.then_inc(bc_done, 1)

            def gate_up(n, u0, ready, ada):
                def body(i, k0):
                    for k in range(k0, 4):
                        pe.wait_ge((silu_done, prod_done)[k % 2][n][k // 2], i + START)
                        h_unit(i * 4 + u0 + k, (u0 + k) % 2, bank[:, k, :]).then_inc(unit_done, 1)
                    if ada:
                        ada_sums(i)

                two_units(u0, (0, 1), ready)
                body(0, 2)
                with pe.Fori(1, FT // 2) as i:
                    body(i, 0)

            def down(n, m, u0, ada):
                def body(i):
                    for k in range(6):
                        k0, cnt = PARTS[k % 3]
                        j = k // 3
                        if k % 3 == 0:
                            pe.wait_ge(x_done[m][j], i + START)
                        pe.wait_ge(actL_done[n], k0 + cnt + START)
                        u = i * 6 + u0 + k
                        pe.wait_ge(lo_done, u + 1 + FREE)
                        for q in range(cnt):
                            f = k0 + q
                            ins = three(bank[:, 5 + j, :], tile((u0 + k) % 2, q), (actH[:, f, :], actL[:, f, :]),
                                        f == 0, f == FT - 1)
                        ins.then_inc(unit_done, 1)
                        if ada and isinstance(i, int) and k == 1:
                            pe.wait_ge(modrows_in, 16)
                            pe.wait_ge(mod_done, ADA1 + START)
                            rows = ADA1 * AC // P
                            T.transpose(bank[:, B_ADA, :rows], modrows, ident[:rows, :rows]).then_inc(ada_sum, 1)

                if ada:
                    body(0)
                with pe.Fori(int(ada), DT // 2) as i:
                    body(i)

            def pairs(br):
                u0 = U_MIX[br]
                def body(i, q_made=False):
                    for pp in range(2):
                        g = i * 2 + (4 * br + pp)
                        k0 = 5 * pp

                        def unit(k, b, ks=range(DT)):
                            return h_unit(i * 10 + u0 + k0 + k, (u0 + k0 + k) % 2, bank[:, b, :], ks)

                        def flat(hh):
                            return bank[:, S_BANK[hh]:S_BANK[hh] + 3, :].rearrange("p a b -> p (a b)")

                        def scores():
                            for hh in range(2):
                                pe.wait_ge(o_ready[hh], g + START)
                            for t in T_ORDER:
                                w = P * (t + 1)
                                cols = slice(t * P, (t + 1) * P)
                                for hh in range(2):
                                    o = flat(hh)[:, T_OFF[t]:T_OFF[t] + w]
                                    T.matmul(o, qHH[:, hh, cols], kHL[:, hh, :w], start=True, stop=False)
                                    T.matmul(o[:, w - P:], identb[:, :], mask[br][:, :], start=False, stop=False)
                                for hh in range(2):
                                    o = flat(hh)[:, T_OFF[t]:T_OFF[t] + w]
                                    T.matmul(o, qL[head_rows(hh), cols], kHL[head_rows(hh), hh, :w], start=False, stop=True).then_inc(s_done, 1)

                        def turn(hh):
                            pe.wait_ge(p_ready, g * 8 + (4 * hh + 4))
                            for piece in J_PIECES:
                                for j in piece:
                                    for t in range(j, TT):
                                        ins = T.transpose(flat(hh)[:, J_OFF[j] + (t - j) * P:J_OFF[j] + (t - j + 1) * P],
                                                          prob[:, hh, T_OFF[t] + j * P:T_OFF[t] + (j + 1) * P], ident[:, :])
                                ins.then_inc(p_turned, 1)

                        def values(hh):
                            pe.wait_ge(d_free[1], g * 5 + 4 + START)
                            for j in range(TT):
                                if j < 2:
                                    pe.wait_ge(pt_ready, g * 4 + (2 * hh + j + 1))
                                w = SEQ - j * P
                                o = bank[:, S_BANK[hh], j * P:SEQ]
                                pt = slice(J_OFF[j], J_OFF[j] + w)
                                T.matmul(o, vHL[:, hh, j, :], ptH[:, pt], start=j == 0, stop=False)
                                ins = T.matmul(o, vHL[:, hh, j, :], ptL[:, pt], start=False, stop=j == TT - 1)
                            ins.then_inc(pv_done, 1)

                        if not (q_made and pp == 0):
                            pe.wait_ge(d_free[0], g * 3 + 1)
                            unit(0, 0).then_inc(unit_done, 1)
                        pe.wait_ge(d_free[1], g * 5 + START)
                        unit(1, 1).then_inc(unit_done, 1)
                        pe.wait_ge(d_free[0], g * 3 + 3)
                        unit(2, 0).then_inc(unit_done, 1)
                        pe.wait_ge(d_free[1], g * 5 + 2 + START)
                        if br == 1:
                            pe.wait_ge(y_done, DT + Y_START)
                        scores()
                        pe.wait_ge(v_copied, g + 1)
                        for t in range(TT):
                            ins = T.transpose(bank[:, 1, t * P:(t + 1) * P], vT[:, t * P:(t + 1) * P], ident[:, :])
                        ins.then_inc(v_turned, 1)
                        unit(3, 0).then_inc(unit_done, 1)
                        turn(0)
                        pe.wait_ge(d_free[1], g * 5 + 4 + START)
                        unit(4, 1, range(0, DT // 2))
                        values(0)
                        turn(1)
                        unit(4, 1, range(DT // 2, DT)).then_inc(unit_done, 1)
                        values(1)

                if br == 0:
                    body(0, True)
                with pe.Fori(1 - br, PAIRS // 2) as i:
                    body(i)

            def branch(br):
                u0 = U_BR[br]
                for hh in range(2):
                    pe.wait_ge(o_ready[hh], PAIRS * (br + 1) - hh + START)
                with pe.Fori(0, DT // 4) as i:
                    for k in range(2):
                        s = (u0 + k) % 2
                        pe.wait_ge(y_done, i * 4 + (br * DT - 2 + 2 * k) + Y_START)
                        pe.wait_ge(lo_done, i * 2 + u0 + k + 1 + FREE)
                        for q, e in [(q, e) for q in range(PAIRS) for e in range(2)]:
                            if k == e == 0 and q == PAIRS - 1:
                                pe.wait_ge(o_ready[1], PAIRS * (br + 1) + START)
                            cols = slice((q * 2 + e) * P, (q * 2 + e + 1) * P)
                            ins = three(bank[:, 2 + 2 * k + e, :], (wH[s][:, cols], wL[s][:, cols]),
                                        (oH[:, q, :], oL[:, q, :]), q == 0, q == PAIRS - 1)
                        ins.then_inc(unit_done, 1)

            for first in (s_done, pv_done):
                pe.sem_inc(first, START)
            pe.wait_ge(ident_made, 1)
            pe.wait_ge(prm_loaded, 16 * 6)
            T.transpose(bank[:, 0, :N_PRM], prm_in[:N_PRM, :], ident[:N_PRM, :N_PRM]).then_inc(prm_T, 1)
            pe.wait_ge(c_act, 1)
            first_parts(0)
            first_sums(0)
            for t in range(TT):
                pe.wait_ge(x_in[t], 16)
            for d in range(DT):
                if d >= 2:
                    pe.wait_ge(xt_done, d - 1)
                for t in range(TT):
                    ins = T.transpose(bank[:, 1 + d % 2, t * P:(t + 1) * P], xin[:, t, d * P:(d + 1) * P], ident[:, :])
                ins.then_inc(xt_psum, 1)
            first_parts(1)
            spread(0)
            pe.wait_ge(onesr_made, 1)
            first_sums(1)
            gate_up(0, U_GU1, 0, True)
            down(0, 0, U_DN1, True)
            last_sums(range(0, 8))
            token_squares(0)
            last_sums(range(8, N_LAST)).then_inc(ada_sum, 1)
            spread(1)
            two_units(U_FA, (B_FA, 0), DT)
            pe.wait_ge(identb_made, 1)
            pe.wait_ge(masks_made, 2)
            pairs(0)
            branch(0)
            pairs(1)
            branch(1)
            with pe.Fori(0, DT // 2) as i:
                for k in range(2):
                    pe.wait_ge(x_done[1][k], i + START)
                    if k == 0:
                        pe.wait_ge(lo_done, i * 2 + U_OUT + k + 1 + FREE)
                        for q in range(DT):
                            pe.wait_ge(yH_ready, q + 1)
                            ins = three(bank[:, k, :], tile((U_OUT + k) % 2, q), (hH[:, q, :], hL[:, q, :]),
                                        q == 0, q == DT - 1)
                    else:
                        ins = h_unit(i * 2 + U_OUT + k, (U_OUT + k) % 2, bank[:, k, :])
                    ins.then_inc(unit_done, 1)
            token_squares(1)
            spread(2)
            gate_up(1, U_GU2, 2 * DT, False)
            down(1, 2, U_DN2, False)
            def turned_out(e, t):
                for q in range(4):
                    ins = T.transpose(bank[:, Y_BANK[e][t], q * P:(q + 1) * P], xg[:, 4 * e + q, t * P:(t + 1) * P], ident[:, :])
                ins.then_inc(yt_done[e], 1)

            pe.wait_ge(xg_done, 4)
            for t in range(TT):
                turned_out(0, t)
            token_squares(2)
            pe.wait_ge(xg_done, DT)
            for t in range(TT):
                if t == TT - 1:
                    pe.wait_ge(y_ready[0], 1)
                turned_out(1, t)


_INS = ['x', 'c', 'ada_w', 'ada_b', 'norm_ffn1', 'ffn1_w_gate', 'ffn1_w_up', 'ffn1_w_down', 'norm_mix', 'mix_w_in',
        'forget_b', 'branch_gate_b', 'rel_bias', 'branch_w_a', 'branch_w_b', 'mix_w_out', 'norm_ffn2', 'ffn2_w_gate',
        'ffn2_w_up', 'ffn2_w_down', 'final_norm']
_OUTS = [((1, 512, 1024), 'float32')]


def kernel(**inputs):
    import numpy as _np
    import concourse.bacc as _bacc
    from concourse import mybir as _mybir
    from concourse.bass_utils import run_bass_kernel_spmd as _run

    nc = _bacc.Bacc("TRN2", target_bir_lowering=False, num_devices=1)
    arrays, args = {}, []
    for name in _INS:
        a = _np.ascontiguousarray(inputs[name])
        arrays[f"in_{name}_dram"] = a
        args.append(nc.dram_tensor(f"in_{name}_dram", a.shape, _mybir.dt.from_np(a.dtype), kind="ExternalInput").ap())
    for i, (shape, dtype) in enumerate(_OUTS):
        dt = _mybir.dt.from_np(_np.dtype(dtype))
        args.append(nc.dram_tensor(f"out_{i}_dram", shape, dt, kind="ExternalOutput").ap())
    hybrid_block(nc, *args)
    r = _run(nc, [arrays], core_ids=[0])
    return r.results[0]["out_0_dram"]
```
